# Optimizing a Trainium2 kernel written in Bass

```python
import jax, jax.numpy as jnp
from jax import lax
import numpy as np
import math

D_MODEL = 1024
BATCH = 1
SEQ = 512
DEPTH = 1

GRID_W = 64
HEAD_DIM = 64
A_HEADS = D_MODEL // (2 * HEAD_DIM)
A_KV_HEADS = A_HEADS // 4
A_WINDOW = 128
A_BLOCK = 128
B_HEADS = D_MODEL // (2 * HEAD_DIM)
B_KH_MAX = 8
B_KW = 16
D_FF = 4 * D_MODEL
EPS = 1e-6
A_WIDTH = A_HEADS * HEAD_DIM
A_KV_WIDTH = A_KV_HEADS * HEAD_DIM
B_WIDTH = B_HEADS * HEAD_DIM
IN_WIDTH = A_WIDTH + 2 * A_KV_WIDTH + 3 * B_WIDTH + 2 * D_MODEL


def rms_norm(x, g):
    xf = x.astype(jnp.float32)
    var = jnp.mean(xf * xf, axis=-1, keepdims=True)
    return (xf * lax.rsqrt(var + EPS)).astype(x.dtype) * g

def alibi_slopes(n):
    return 2.0 ** (-8.0 * jnp.arange(1, n + 1, dtype=jnp.float32) / n)

def windowed_gqa(q, k, v, sink):
    b, s, _, d = q.shape
    nb = s // A_BLOCK
    grp = A_HEADS // A_KV_HEADS
    qb = q.reshape(b, nb, A_BLOCK, A_KV_HEADS, grp, d)
    pad = ((0, 0), (A_BLOCK, A_BLOCK), (0, 0), (0, 0))
    kp = jnp.pad(k, pad)
    vp = jnp.pad(v, pad)
    slopes = alibi_slopes(A_HEADS).reshape(A_KV_HEADS, grp)
    sink_f = sink.astype(jnp.float32).reshape(A_KV_HEADS, grp)
    scale = d ** -0.5

    def block(i):
        qi = qb[:, i]
        ki = lax.dynamic_slice_in_dim(kp, i * A_BLOCK, 3 * A_BLOCK, axis=1)
        vi = lax.dynamic_slice_in_dim(vp, i * A_BLOCK, 3 * A_BLOCK, axis=1)
        q_pos = i * A_BLOCK + jnp.arange(A_BLOCK)
        k_pos = (i - 1) * A_BLOCK + jnp.arange(3 * A_BLOCK)
        dist = jnp.abs(q_pos[:, None] - k_pos[None, :])
        valid = (dist <= A_WINDOW) & (k_pos[None, :] >= 0) & (k_pos[None, :] < s)
        sc = jnp.einsum('bqkgd,bskd->bkgqs', qi, ki).astype(jnp.float32) * scale
        sc = sc - slopes[:, :, None, None] * dist.astype(jnp.float32)
        sc = jnp.where(valid, sc, -jnp.inf)
        sink_col = jnp.broadcast_to(sink_f[None, :, :, None, None], sc.shape[:-1] + (1,))
        p = jax.nn.softmax(jnp.concatenate([sc, sink_col], axis=-1), axis=-1)[..., :-1]
        return jnp.einsum('bkgqs,bskd->bqkgd', p.astype(v.dtype), vi)

    out = lax.map(block, jnp.arange(nb))
    return jnp.moveaxis(out, 0, 1).reshape(b, s, A_WIDTH)

def neighborhood_attn(q, k, v, rpb):
    b, s, h, d = q.shape
    rows = s // GRID_W
    kh = min(B_KH_MAX, rows)
    qg = q.reshape(b, rows, GRID_W, h, d)
    kg = k.reshape(b, rows, GRID_W, h, d)
    vg = v.reshape(b, rows, GRID_W, h, d)
    cols = jnp.arange(GRID_W)
    col_start = jnp.clip(cols - B_KW // 2, 0, GRID_W - B_KW)
    col_idx = col_start[:, None] + jnp.arange(B_KW)[None, :]
    dc = col_idx - cols[:, None] + (B_KW - 1)
    rpb_f = rpb.astype(jnp.float32)
    scale = d ** -0.5

    def row(r):
        r0 = jnp.clip(r - kh // 2, 0, rows - kh)
        kr = lax.dynamic_slice_in_dim(kg, r0, kh, axis=1)
        vr = lax.dynamic_slice_in_dim(vg, r0, kh, axis=1)
        kn = kr[:, :, col_idx]
        vn = vr[:, :, col_idx]
        qr = lax.dynamic_index_in_dim(qg, r, axis=1, keepdims=False)
        sc = jnp.einsum('bchd,brckhd->bhcrk', qr, kn).astype(jnp.float32) * scale
        dr = r0 + jnp.arange(kh) - r + (B_KH_MAX - 1)
        bias = rpb_f[:, dr[:, None, None], dc[None, :, :]]
        sc = sc + jnp.transpose(bias, (0, 2, 1, 3))[None]
        p = jax.nn.softmax(sc.reshape(b, h, GRID_W, kh * B_KW), axis=-1)
        p = p.reshape(b, h, GRID_W, kh, B_KW).astype(v.dtype)
        return jnp.einsum('bhcrk,brckhd->bchd', p, vn)

    out = lax.map(row, jnp.arange(rows))
    return jnp.moveaxis(out, 0, 1).reshape(b, s, B_WIDTH)

def first_inputs(seed: int = 0) -> dict:
    key = jax.random.key(seed)
    ks = jax.random.split(key, 14)
    f32 = jnp.float32

    def nrm(k, shape, scale):
        return jax.random.normal(k, shape, f32) * scale

    return {
        "x": nrm(ks[0], (BATCH, SEQ, D_MODEL), 1.0),
        "norm_mix": 1.0 + nrm(ks[1], (DEPTH, D_MODEL), 0.02),
        "w_in": nrm(ks[2], (DEPTH, D_MODEL, IN_WIDTH), D_MODEL ** -0.5),
        "b_gate": nrm(ks[3], (DEPTH, 2 * D_MODEL), 0.01),
        "sink": nrm(ks[4], (DEPTH, A_HEADS), 0.5),
        "rpb": nrm(ks[5], (DEPTH, B_HEADS, 2 * B_KH_MAX - 1, 2 * B_KW - 1), 0.1),
        "w_proj_a": nrm(ks[6], (DEPTH, A_WIDTH, D_MODEL), A_WIDTH ** -0.5),
        "w_proj_b": nrm(ks[7], (DEPTH, B_WIDTH, D_MODEL), B_WIDTH ** -0.5),
        "w_out": nrm(ks[8], (DEPTH, D_MODEL, D_MODEL), D_MODEL ** -0.5),
        "norm_mlp": 1.0 + nrm(ks[9], (DEPTH, D_MODEL), 0.02),
        "w_up": nrm(ks[10], (DEPTH, D_MODEL, D_FF), D_MODEL ** -0.5),
        "w_down": nrm(ks[11], (DEPTH, D_FF, D_MODEL), D_FF ** -0.5),
        "norm_final": 1.0 + nrm(ks[12], (D_MODEL,), 0.02),
    }

def first_block(x, norm_mix, w_in, b_gate, sink, rpb, w_proj_a, w_proj_b, w_out,
              norm_mlp, w_up, w_down, norm_final):
    b, s, _ = x.shape
    sizes = [A_WIDTH, A_KV_WIDTH, A_KV_WIDTH, B_WIDTH, B_WIDTH, B_WIDTH, D_MODEL, D_MODEL]
    offsets = [int(o) for o in np.cumsum(sizes)[:-1]]
    for l in range(DEPTH):
        h = rms_norm(x, norm_mix[l])
        z = h @ w_in[l]
        q_a, k_a, v_a, q_b, k_b, v_b, g_a, g_b = jnp.split(z, offsets, axis=-1)
        y_a = windowed_gqa(q_a.reshape(b, s, A_HEADS, HEAD_DIM),
                           k_a.reshape(b, s, A_KV_HEADS, HEAD_DIM),
                           v_a.reshape(b, s, A_KV_HEADS, HEAD_DIM), sink[l])
        y_b = neighborhood_attn(q_b.reshape(b, s, B_HEADS, HEAD_DIM),
                                k_b.reshape(b, s, B_HEADS, HEAD_DIM),
                                v_b.reshape(b, s, B_HEADS, HEAD_DIM), rpb[l])
        gates = jax.nn.sigmoid((jnp.concatenate([g_a, g_b], axis=-1) + b_gate[l])
                               .astype(jnp.float32)).astype(x.dtype)
        merged = (gates[..., :D_MODEL] * (y_a @ w_proj_a[l])
                  + gates[..., D_MODEL:] * (y_b @ w_proj_b[l]))
        x = x + merged @ w_out[l]
        h2 = rms_norm(x, norm_mlp[l])
        x = x + jnp.square(jax.nn.relu(h2 @ w_up[l])) @ w_down[l]
    return rms_norm(x, norm_final)


DEPTH_2 = 2

N_Q_HEADS = 8
N_KV_HEADS = 2
GQA_GROUP = N_Q_HEADS // N_KV_HEADS
ATTN_WIDTH = N_Q_HEADS * HEAD_DIM
KV_WIDTH = N_KV_HEADS * HEAD_DIM
N_CONV_GROUPS = 8
CONV_WIDTH = N_CONV_GROUPS * HEAD_DIM
MIX_WIDTH = ATTN_WIDTH + CONV_WIDTH
CONV_K = 3
WINDOW = 128
BLOCK = 128
D_FF_2 = 2816
NORM_EPS = 1e-6

Q_END = ATTN_WIDTH
K_END = Q_END + KV_WIDTH
V_END = K_END + KV_WIDTH
CB_END = V_END + CONV_WIDTH
CC_END = CB_END + CONV_WIDTH
CH_END = CC_END + CONV_WIDTH
IN_WIDTH_2 = CH_END


def rms_norm_2(x, gain):
    xf = x.astype(jnp.float32)
    inv = lax.rsqrt(jnp.mean(xf * xf, axis=-1, keepdims=True) + NORM_EPS)
    return (xf * inv).astype(x.dtype) * gain

def swiglu(h, w_gate, w_up, w_down):
    return (jax.nn.silu(h @ w_gate) * (h @ w_up)) @ w_down

def alibi_slopes_2(n_heads):
    return jnp.exp2(-8.0 * jnp.arange(1, n_heads + 1, dtype=jnp.float32) / n_heads)

def short_conv(b_gate, c_gate, h_conv, conv_w):
    u = c_gate * h_conv
    w = conv_w.astype(u.dtype)[:, None, :]
    y = lax.conv_general_dilated(
        u, w, window_strides=(1,), padding=[(CONV_K - 1, 0)],
        dimension_numbers=("NWC", "WIO", "NWC"), feature_group_count=CONV_WIDTH)
    return b_gate * y

def sliding_window_attention(q, k, v, sink):
    bsz, seq = q.shape[0], q.shape[1]
    nb = seq // BLOCK
    qb = q.reshape(bsz, nb, BLOCK, N_KV_HEADS, GQA_GROUP, HEAD_DIM)
    kb = k.reshape(bsz, nb, BLOCK, N_KV_HEADS, HEAD_DIM)
    vb = v.reshape(bsz, nb, BLOCK, N_KV_HEADS, HEAD_DIM)
    pad = ((0, 0), (1, 0), (0, 0), (0, 0), (0, 0))
    k_band = jnp.concatenate([jnp.pad(kb, pad)[:, :-1], kb], axis=2)
    v_band = jnp.concatenate([jnp.pad(vb, pad)[:, :-1], vb], axis=2)

    scale = 1.0 / math.sqrt(HEAD_DIM)
    scores = jnp.einsum("bnqkgd,bnskd->bnkgqs", qb, k_band).astype(jnp.float32) * scale

    qi = jnp.arange(BLOCK)[:, None]
    kj = jnp.arange(2 * BLOCK)[None, :]
    dist = qi + BLOCK - kj
    in_window = (dist >= 0) & (dist < WINDOW)
    blk = jnp.arange(nb)[:, None, None]
    mask = in_window[None] & ((blk > 0) | (kj[None] >= BLOCK))

    slopes = alibi_slopes_2(N_Q_HEADS).reshape(N_KV_HEADS, GQA_GROUP)
    bias = -slopes[:, :, None, None] * dist.astype(jnp.float32)[None, None]
    scores = scores + bias[None, None]
    mask_b = mask[None, :, None, None]
    scores = jnp.where(mask_b, scores, -jnp.inf)

    sink_l = sink.astype(jnp.float32).reshape(1, 1, N_KV_HEADS, GQA_GROUP, 1, 1)
    m = jnp.maximum(jnp.max(scores, axis=-1, keepdims=True), sink_l)
    p = jnp.where(mask_b, jnp.exp(scores - m), 0.0)
    denom = jnp.sum(p, axis=-1, keepdims=True) + jnp.exp(sink_l - m)
    probs = (p / denom).astype(v.dtype)
    out = jnp.einsum("bnkgqs,bnskd->bnqkgd", probs, v_band)
    return out.reshape(bsz, seq, ATTN_WIDTH)

def second_inputs(seed: int = 0) -> dict:
    key = jax.random.key(seed)
    ks = jax.random.split(key, 20)
    f32 = jnp.float32

    def w(k, shape, fan_in):
        return jax.random.normal(k, shape, f32) * (fan_in ** -0.5)

    def gain(k, shape):
        return 1.0 + 0.05 * jax.random.normal(k, shape, f32)

    return {
        "x": jax.random.normal(ks[0], (BATCH, SEQ, D_MODEL), f32),
        "ffn1_norm": gain(ks[1], (DEPTH_2, D_MODEL)),
        "ffn1_wg": w(ks[2], (DEPTH_2, D_MODEL, D_FF_2), D_MODEL),
        "ffn1_wu": w(ks[3], (DEPTH_2, D_MODEL, D_FF_2), D_MODEL),
        "ffn1_wd": w(ks[4], (DEPTH_2, D_FF_2, D_MODEL), D_FF_2),
        "mix_norm": gain(ks[5], (DEPTH_2, D_MODEL)),
        "w_in": w(ks[6], (DEPTH_2, D_MODEL, IN_WIDTH_2), D_MODEL),
        "conv_w": w(ks[7], (DEPTH_2, CONV_K, CONV_WIDTH), CONV_K),
        "attn_sink": 0.5 * jax.random.normal(ks[8], (DEPTH_2, N_Q_HEADS), f32),
        "w_out": w(ks[9], (DEPTH_2, MIX_WIDTH, D_MODEL), MIX_WIDTH),
        "ffn2_norm": gain(ks[10], (DEPTH_2, D_MODEL)),
        "ffn2_wg": w(ks[11], (DEPTH_2, D_MODEL, D_FF_2), D_MODEL),
        "ffn2_wu": w(ks[12], (DEPTH_2, D_MODEL, D_FF_2), D_MODEL),
        "ffn2_wd": w(ks[13], (DEPTH_2, D_FF_2, D_MODEL), D_FF_2),
        "final_norm": gain(ks[14], (D_MODEL,)),
    }

def second_block(x, ffn1_norm, ffn1_wg, ffn1_wu, ffn1_wd, mix_norm, w_in, conv_w,
              attn_sink, w_out, ffn2_norm, ffn2_wg, ffn2_wu, ffn2_wd, final_norm):
    bsz, seq, _ = x.shape
    for l in range(DEPTH_2):
        x = x + 0.5 * swiglu(rms_norm_2(x, ffn1_norm[l]), ffn1_wg[l], ffn1_wu[l], ffn1_wd[l])

        h = rms_norm_2(x, mix_norm[l])
        z = h @ w_in[l]
        q = z[..., :Q_END].reshape(bsz, seq, N_Q_HEADS, HEAD_DIM)
        k = z[..., Q_END:K_END].reshape(bsz, seq, N_KV_HEADS, HEAD_DIM)
        v = z[..., K_END:V_END].reshape(bsz, seq, N_KV_HEADS, HEAD_DIM)
        attn_out = sliding_window_attention(q, k, v, attn_sink[l])
        conv_out = short_conv(z[..., V_END:CB_END], z[..., CB_END:CC_END],
                              z[..., CC_END:CH_END], conv_w[l])
        x = x + jnp.concatenate([attn_out, conv_out], axis=-1) @ w_out[l]

        x = x + 0.5 * swiglu(rms_norm_2(x, ffn2_norm[l]), ffn2_wg[l], ffn2_wu[l], ffn2_wd[l])
    return rms_norm_2(x, final_norm)


def setup_inputs(seed=0):
    out = dict(first_inputs(seed))
    for name, value in second_inputs(seed + 1).items():
        if name != "x":
            out[name + "_2"] = value
    return out


def reference(
    x, norm_mix, w_in, b_gate, sink, rpb, w_proj_a, w_proj_b, w_out, norm_mlp, w_up, w_down,
    norm_final, ffn1_norm_2, ffn1_wg_2, ffn1_wu_2, ffn1_wd_2, mix_norm_2, w_in_2, conv_w_2,
    attn_sink_2, w_out_2, ffn2_norm_2, ffn2_wg_2, ffn2_wu_2, ffn2_wd_2, final_norm_2,
):
    x = first_block(
        x, norm_mix, w_in, b_gate, sink, rpb, w_proj_a, w_proj_b, w_out, norm_mlp, w_up, w_down,
        norm_final,
    )
    return second_block(
        x, ffn1_norm_2, ffn1_wg_2, ffn1_wu_2, ffn1_wd_2, mix_norm_2, w_in_2, conv_w_2,
        attn_sink_2, w_out_2, ffn2_norm_2, ffn2_wg_2, ffn2_wu_2, ffn2_wd_2, final_norm_2,
    )


_drawn_inputs = setup_inputs


def setup_inputs(seed=0):
    import zlib

    import numpy as np

    out = dict(_drawn_inputs(seed))
    spreads = {}
    factors = {'norm_mix': 5.75,
     'b_gate': 21.407,
     'sink': 8.0,
     'rpb': 4.143,
     'attn_sink_2': 3.43,
     'norm_mlp': 6.297}
    for name, (base, spread) in spreads.items():
        noise = np.random.default_rng([zlib.crc32(name.encode()), seed]).standard_normal(out[name].shape)
        drawn = base * np.exp(spread * noise) if base else spread * noise
        out[name] = __import__('jax').numpy.asarray(drawn.astype(out[name].dtype))
    for name, factor in factors.items():
        out[name] = (out[name] * factor).astype(out[name].dtype)
    return out
```

```python
from contextlib import ExitStack

import numpy as np
import concourse.bass as bass
from concourse import mybir

F32 = mybir.dt.float32
F32R = mybir.dt.float32r
ALU = mybir.AluOpType
ACT = mybir.ActivationFunctionType
AX_X = mybir.AxisListType.X

P = 128
TOKENS = 512
D_MODEL = 1024
HEAD = 64
HEADS = 8
KV_HEADS = 2
GROUP = HEADS // KV_HEADS
BLOCK = 128
BLOCKS = TOKENS // BLOCK
KT = D_MODEL // P
FF_CHUNK = 8
FF1_TILES = 4096 // P
FF2_TILES = 2816 // P
LAYERS_2 = 2
EPS = 1e-6
SCALE = HEAD ** -0.5
MASKED = 1e30
UNIT = KT * P
GRID_W = 64
GRID_R = TOKENS // GRID_W
WIN_W = 16
BLOCK_C = BLOCK // GRID_R
SPAN_C = 2 * BLOCK_C
REL_R = 15
REL_C = 31
REL_PAD = (BLOCK_C - 1 + SPAN_C) * GRID_R


class Semaphore:

    def __init__(self, handle):
        self.handle, self.value = handle, 0

    def next(self, amount):
        self.value += amount
        return (self, self.value)


class Queues:

    def __init__(self, engines):
        self.todo = {name: [] for name in engines}
        self.seen = {name: {} for name in engines}
        self.done = {}

    def wait(self, engine, *tokens):
        for token in tokens:
            if token is None:
                continue
            semaphore, value = token
            if value <= self.seen[engine].get(semaphore, 0):
                continue
            self.seen[engine][semaphore] = value
            self.todo[engine].append(lambda e, h=semaphore.handle, v=value: e.wait_ge(h, v))

    def issue(self, engine, make, after=(), signal=True):
        self.wait(engine, *after)
        if not signal:
            self.todo[engine].append(make)
            return None
        token = self.done[engine].next(1)
        self.todo[engine].append(lambda e, h=token[0].handle: make(e).then_inc(h, 1))
        return token

    def dma(self, engine, make, semaphore, after=()):
        self.wait(engine, *after)
        token = semaphore.next(16)
        self.todo[engine].append(lambda e, h=semaphore.handle: make(e).then_inc(h, 16))
        return token


class Ring:

    def __init__(self, buffers):
        self.buffers, self.users, self.at = list(buffers), [()] * len(buffers), -1

    def take(self):
        self.at = (self.at + 1) % len(self.buffers)
        return self.at, self.buffers[self.at], self.users[self.at]

    def release(self, slot, *tokens):
        self.users[slot] = tokens


def two_blocks(nc, dram, out):
    engines = ("tensor", "vector", "scalar", "gpsimd", "sync")
    q = Queues(engines)
    stack = ExitStack()
    with stack:
        def sbuf(name, shape, dt=F32, on=stack):
            return on.enter_context(nc.sbuf_tensor(name, shape, dt))

        def semaphore(name):
            return Semaphore(stack.enter_context(nc.semaphore(name)))

        x = sbuf("x", [P, KT, TOKENS])
        h_hi = sbuf("h_hi", [P, KT, TOKENS], F32R)
        h_lo = sbuf("h_lo", [P, KT, TOKENS], F32R)
        n_units = 3
        w_raw = [sbuf(f"w_raw{i}", [P, UNIT]) for i in range(n_units)]
        w_hi = [sbuf(f"w_hi{i}", [P, UNIT], F32R) for i in range(n_units)]
        w_lo = [sbuf(f"w_lo{i}", [P, UNIT], F32R) for i in range(n_units)]
        rms_inv = sbuf("rms_inv", [P, TOKENS])
        square_sum = sbuf("square_sum", [P, TOKENS])
        temps = Ring([sbuf(f"temp{i}", [P, TOKENS]) for i in range(5)])
        identity = sbuf("identity", [P, P])
        ones = sbuf("ones", [P, P])
        dist_1 = sbuf("dist_1", [P, 3 * BLOCK])
        dist_2 = sbuf("dist_2", [P, 2 * BLOCK])
        eps_col = sbuf("eps_col", [P, 1])
        gains = sbuf("gains", [P, 10, KT])
        gain_product = sbuf("gain_product", [P, KT])
        gate_bias = sbuf("gate_bias", [P, 2 * KT])
        sinks = sbuf("sinks", [P, 3, HEADS])
        sinks_8 = sbuf("sinks_8", [P, 3, HEADS])
        conv_w = sbuf("conv_w", [P, LAYERS_2, 4, 3])
        row_max = sbuf("row_max", [P, 2, HEADS])
        neg_max = sbuf("neg_max", [P, 2, HEADS])
        sink_shift = sbuf("sink_shift", [P, 2, HEADS])
        sink_exp = sbuf("sink_exp", [P, 2, HEADS])
        row_sum = sbuf("row_sum", [P, 2, HEADS])
        row_inv = sbuf("row_inv", [P, 2, HEADS])

        def phase(tensors, on):
            return [sbuf(n, s, d, on) for n, s, d in tensors]

        ff_phase, mix1, mix2 = ExitStack(), ExitStack(), ExitStack()
        ff_ring = FF_CHUNK + 2
        with ff_phase:
            act_hi, act_lo = phase([("act_hi", [P, ff_ring, TOKENS], F32R), ("act_lo", [P, ff_ring, TOKENS], F32R)], ff_phase)
            scaled_square_sum, rms_first = phase([("scaled_square_sum", [P, TOKENS], F32), ("rms_first", [P, TOKENS], F32)], ff_phase)
        with mix1:
            qa_hi, qa_lo = phase([("qa_hi", [P, 4, TOKENS], F32R), ("qa_lo", [P, 4, TOKENS], F32R)], mix1)
            qb_hi, qb_lo = phase([("qb_hi", [P, 4, TOKENS], F32R), ("qb_lo", [P, 4, TOKENS], F32R)], mix1)
            probs_t1, out_q1, probs_1 = phase([
                ("probs_t1", [P, 2, TOKENS], F32), ("out_q1", [P, TOKENS], F32),
                ("probs_1", [P, 3, GROUP, 3 * BLOCK], F32)], mix1)
            with ExitStack() as kv_part:
                kb_hi, kb_lo = phase([("kb_hi", [P, 4, TOKENS], F32R), ("kb_lo", [P, 4, TOKENS], F32R)], kv_part)
                (vb,) = phase([("vb", [P, BLOCKS + 1, HEADS, HEAD], F32)], kv_part)
                rel_bias, masked_bias = phase([("rel_bias", [P, HEADS, 2 * BLOCK], F32),
                                               ("masked_bias", [P, HEADS, 2 * BLOCK], F32)], kv_part)
                with ExitStack() as part_a:
                    ka_hi, ka_lo, va = phase([("ka_hi", [P, TOKENS], F32R), ("ka_lo", [P, TOKENS], F32R),
                                              ("va", [P, BLOCKS, KV_HEADS, HEAD], F32)], part_a)
                with ExitStack() as part_b:
                    (gates,) = phase([("gates", [P, 2, TOKENS], F32)], part_b)
            with ExitStack() as part_m:
                mg_hi, mg_lo, gates_b = phase([("mg_hi", [P, KT, TOKENS], F32R), ("mg_lo", [P, KT, TOKENS], F32R),
                                               ("gates_b", [P, 2, TOKENS], F32)], part_m)
        with mix2:
            q2_hi, q2_lo = phase([("q2_hi", [P, 4, TOKENS], F32R), ("q2_lo", [P, 4, TOKENS], F32R)], mix2)
            k2_hi, k2_lo, v2 = phase([("k2_hi", [P, TOKENS], F32R), ("k2_lo", [P, TOKENS], F32R),
                                      ("v2", [P, BLOCKS, KV_HEADS, HEAD], F32)], mix2)
            probs_t2, out_q2, probs_2 = phase([
                ("probs_t2", [P, 2, TOKENS], F32), ("out_q2", [P, TOKENS], F32),
                ("probs_2", [P, 3, GROUP, 2 * BLOCK], F32)], mix2)
            cv_hi, cv_lo = phase([("cv_hi", [P, 4, TOKENS], F32R), ("cv_lo", [P, 4, TOKENS], F32R)], mix2)
            conv_c, conv_u, conv_y = phase([("conv_c", [P, TOKENS], F32), ("conv_u", [P, TOKENS + 2], F32),
                                            ("conv_y", [P, TOKENS], F32)], mix2)

        psum = [stack.enter_context(nc.psum_tensor(f"bank{i}", [P, TOKENS], F32)) for i in range(8)]
        dense_banks, score_banks, turn_banks = Ring(psum[0:3]), Ring(psum[3:5]), Ring(psum[5:7])
        value_bank = Ring(psum[7:8])

        for name in engines[:4]:
            q.done[name] = semaphore(f"{name}_done")
        landed = [semaphore(f"weights_landed{i}") for i in range(n_units)]
        consts_landed = [semaphore(f"consts_landed{i}") for i in range(8)]
        x_landed = [semaphore(f"x_landed{i}") for i in range(KT)]
        x_back = [semaphore(f"x_back{i}") for i in range(KT)]
        rel_landed = semaphore("rel_landed")
        rel_stored = semaphore("rel_stored")
        bias_landed = semaphore("bias_landed")
        out_stored = semaphore("out_stored")

        def barrier():
            return [(s, s.value) for s in q.done.values() if s.value]

        def load_const(i, dst, src, engine="scalar"):
            return q.dma(engine, lambda e: e.dma_start(dst, src), consts_landed[i])

        gains_in = load_const(0, gains[:, :, :], dram["gains"])
        x_ready = [q.dma("scalar", lambda e, m=m: e.dma_start(x[:, m, :], dram["x"][m * P:(m + 1) * P, :]), x_landed[m])
                   for m in range(KT)]
        dist1_in = load_const(1, dist_1[:, :], dram["dist_1"])
        dist2_in = load_const(2, dist_2[:, :], dram["dist_2"])
        identity_in = load_const(3, identity[:, :], dram["identity"])
        gate_bias_in = load_const(4, gate_bias[:, :], dram["gate_bias"])
        sinks_in = load_const(5, sinks[:, :, :], dram["sinks"].partition_broadcast(P))
        conv_w_in = load_const(6, conv_w[:, :, :, :], dram["conv_w"])
        ones_ready = q.issue("vector", lambda e: e.memset(ones[:, :], 1.0))
        eps_ready = q.issue("vector", lambda e: e.memset(eps_col[:, :], EPS))
        sinks8_ready = q.issue("vector", lambda e: e.tensor_scalar(sinks_8[:, :, :], sinks[:, :, :], 1 / SCALE, None, ALU.mult),
                               after=[sinks_in])

        unit_lo_ready = []
        raw_free = [()] * n_units
        split_free = [()] * n_units
        units = plan_units(dram)
        lo_engine = ["vector"]

        def fetch_unit(u):
            s, (src, width) = u % n_units, units[u]
            return q.dma("sync", lambda e: e.dma_start(w_raw[s][:, 0:width], src), landed[s], after=raw_free[s])

        def split_unit(u):
            if u >= len(units):
                return
            s, width = u % n_units, units[u][1]
            raw_here = fetch_unit(u)
            hi = q.issue("scalar", lambda e: e.activation(w_hi[s][:, 0:width], w_raw[s][:, 0:width], ACT.Copy),
                         after=[raw_here, *split_free[s]])
            lo = q.issue(lo_engine[0], lambda e: e.tensor_tensor(w_lo[s][:, 0:width], w_raw[s][:, 0:width],
                                                                 w_hi[s][:, 0:width].bitcast(F32), ALU.subtract),
                         after=[hi, raw_here, *split_free[s]])
            raw_free[s] = (hi, lo)
            unit_lo_ready.append((hi, lo))

        current = [0]
        first_results = []
        beside = {"slot": 0, "steps": []}

        def start_beside(steps):
            beside["slot"], beside["steps"] = 0, sorted(steps, key=lambda s: s[0])

        def next_slot():
            while beside["steps"] and beside["steps"][0][0] <= beside["slot"]:
                beside["steps"].pop(0)[1]()
            beside["slot"] += 1

        def finish_beside():
            while beside["steps"]:
                beside["steps"].pop(0)[1]()

        def dense(k_tiles, columns, act, ready, last_of_unit=True):
            u = current[0]
            slot, bank, bank_free = dense_banks.take()
            q.wait("tensor", *unit_lo_ready[u], *bank_free)
            for k in range(k_tiles):
                q.wait("tensor", *ready(k))
                token = k_step(u, bank, k, k_tiles, columns, act)
                if k < k_tiles - 1:
                    next_slot()
            if last_of_unit:
                next_unit(token)
            next_slot()
            return slot, bank, token

        def k_step(u, bank, k, k_tiles, columns, act):
            s, width = u % n_units, units[u][1] // k_tiles
            hi, lo = act(k)
            lhs = slice(k * width + columns, k * width + columns + P)
            for n, (w, a) in enumerate(((w_hi[s], hi), (w_hi[s], lo), (w_lo[s], hi))):
                first, last = k == 0 and n == 0, k == k_tiles - 1 and n == 2
                token = q.issue("tensor", lambda e, w=w, a=a, first=first, last=last: e.matmul(
                    bank[:, :], w[:, lhs], a, start=first, stop=last), signal=last)
            return token

        def next_unit(token):
            u = current[0]
            split_free[u % n_units] = (token,)
            current[0] += 1
            split_unit(u + n_units)

        def dense_first():
            results = [dense_banks.take() for _ in range(n_units)]
            for k in range(KT):
                h_tile(k, gains[:, 0, k:k + 1])
                if k < n_units - 1:
                    split_unit(k + 1)
            for k in range(KT):
                for u, (_, bank, _) in enumerate(results):
                    q.wait("tensor", *h_ready[k], *(unit_lo_ready[u] if k == 0 else ()))
                    token = k_step(u, bank, k, KT, 0, act_h)
                    if k == KT - 1:
                        first_results.append((results[u][0], bank, token))
                        next_unit(token)
            h_read[0] = (token,)
            for m in range(KT):
                square_tile(m, engine="vector")
            norm_finish()

        def act_h(k):
            return h_hi[:, k, :], h_lo[:, k, :]

        h_ready = [()] * KT
        h_read = [()]
        x_written = [(t,) for t in x_ready]
        rms_state = {"ready": None, "sum": None, "sum_scaled": None}

        pending_norm = [None]

        def dense_h():
            if first_results:
                return first_results.pop(0)
            result = dense(KT, 0, act_h, lambda k: h_ready[k])
            h_read[0] = (result[2],)
            if pending_norm[0]:
                pending_norm[0]()
                pending_norm[0] = None
            return result

        def split_into(value, hi, lo, after, hi_after=(), lo_engine="vector"):
            hi_done = q.issue("scalar", lambda e: e.activation(hi, value, ACT.Copy), after=[*after, *hi_after])
            lo_done = q.issue(lo_engine, lambda e: e.tensor_tensor(lo, value, hi.bitcast(F32), ALU.subtract),
                              after=[hi_done, *after, *hi_after])
            return hi_done, lo_done

        def h_tile(m, gain_column):
            g = gain_column
            after = [*x_written[m], gains_in]
            hi = q.issue("scalar", lambda e: e.activation(h_hi[:, m, :], x[:, m, :], ACT.Copy, scale=g), after=[*after, *h_read[0]])
            lo = q.issue("vector", lambda e: e.scalar_tensor_tensor(h_lo[:, m, :], x[:, m, :], g, h_hi[:, m, :].bitcast(F32),
                                                                    ALU.mult, ALU.subtract), after=[hi, *after, *h_read[0]])
            h_ready[m] = (hi, lo)

        def square_tile(m, into=square_sum, state="sum", scale=1.0, engine="gpsimd"):
            if m == 0:
                rms_state[state] = q.issue("scalar", lambda e: e.activation(into[:, :], x[:, m, :], ACT.Square, scale=scale),
                                           after=[*x_written[m], rms_state[state]])
                return
            slot, temp, free = temps.take()
            squared = q.issue("scalar", lambda e: e.activation(temp[:, :], x[:, m, :], ACT.Square, scale=scale),
                              after=[*x_written[m], *free])
            rms_state[state] = q.issue(engine, lambda e: e.tensor_tensor(into[:, :], into[:, :], temp[:, :], ALU.add),
                                       after=[squared, rms_state[state]])
            temps.release(slot, rms_state[state])

        def norm_tile(m, gain):
            if gain is not None:
                h_tile(m, gains[:, gain, m:m + 1])
            square_tile(m)

        def sum_partitions(ring, state="sum", source=square_sum):
            slot, bank, free = ring.take()
            summed = q.issue("tensor", lambda e: e.matmul(bank[:, :], ones[:, :], source[:, :], start=True, stop=True),
                             after=[rms_state[state], ones_ready, *free])
            rms_state[state] = summed
            return slot, bank, summed

        def inverse_root(dst, value, scale, bias, after, before=()):
            tslot, temp, tfree = temps.take()
            root = q.issue("scalar", lambda e: e.activation(temp[:, :], value, ACT.Sqrt, bias=bias, scale=scale),
                           after=[*after, eps_ready, *tfree])
            done = q.issue("vector", lambda e: e.reciprocal(dst[:, :], temp[:, :]), after=[root, *before])
            temps.release(tslot, done)
            return root, done

        def norm_finish():
            slot, bank, summed = sum_partitions(value_bank)
            root, rms_state["ready"] = inverse_root(rms_inv, bank[:, :], 1 / D_MODEL, eps_col[:, :], [summed], [rms_state["ready"]])
            value_bank.release(slot, root)

        def norm_finish_twice():
            slot1, bank1, summed1 = sum_partitions(value_bank)
            slot2, bank2, summed2 = sum_partitions(turn_banks, "sum_scaled", scaled_square_sum)
            tslot, temp, tfree = temps.take()
            part = q.issue("vector", lambda e: e.tensor_scalar(temp[:, :], bank1[:, :], EPS / D_MODEL, EPS * EPS, ALU.mult, ALU.add),
                           after=[summed1, *tfree])
            value = q.issue("vector", lambda e: e.scalar_tensor_tensor(temp[:, :], bank2[:, :], 1 / D_MODEL, temp[:, :], ALU.mult, ALU.add),
                            after=[summed2, part])
            root, rms_state["ready"] = inverse_root(rms_inv, temp[:, :], 1.0, 0.0, [value], [rms_state["ready"]])
            first_root, rms_state["first"] = inverse_root(rms_first, bank1[:, :], 1 / D_MODEL, eps_col[:, :], [summed1, part])
            value_bank.release(slot1, first_root)
            turn_banks.release(slot2, value)
            temps.release(tslot, root)

        def scaled(result, dst, view=None, after=()):
            slot, bank, done = result
            src, scale = bank[:, :], rms_inv[:, :]
            if view is not None:
                src, scale, dst = view(src), view(scale), dst.rearrange("p (c r) -> p c r", r=GRID_R)
            token = q.issue("vector", lambda e: e.tensor_tensor(dst, src, scale, ALU.mult),
                            after=[done, rms_state["ready"], *after])
            dense_banks.release(slot, token)
            return token

        def by_column(ap):
            return ap.rearrange("p (r c) -> p c r", r=GRID_R)

        def project_split(hi, lo, view=None, after=()):
            result = dense_h()
            slot, temp, free = temps.take()
            z = scaled(result, temp[:, :], view, after=free)
            tokens = split_into(temp[:, :], hi, lo, [z], hi_after=after)
            temps.release(slot, *tokens)
            return tokens

        def project_v(dst, heads, chunks, view=None, after=()):
            result = dense_h()
            slot, temp, free = temps.take()
            z = scaled(result, temp[:, :], view, after=free)
            temps.release(slot, "in use")
            ready = []

            def turn(c0):
                part = chunks[c0:c0 + 4]
                bslot, bank, bfree = turn_banks.take()
                q.wait("tensor", z, identity_in, *bfree)
                for n, (start, rows) in enumerate(part):
                    turned = q.issue("tensor", lambda e, n=n, start=start, rows=rows: e.transpose(
                        bank[0:rows, n * P:(n + 1) * P], temp[:, start:start + rows], identity[:, :]),
                        signal=n == len(part) - 1)
                runs = []
                for n, (_, rows) in enumerate(part):
                    if runs and runs[-1][2] == rows:
                        runs[-1][1] = n + 1
                    else:
                        runs.append([n, n + 1, rows])
                for a, b, rows in runs:
                    src = bank[0:rows, a * P:b * P].rearrange("p (c h d) -> p c h d", c=b - a, h=2)
                    d = dst[0:rows, c0 + a:c0 + b, heads[0]:heads[0] + 2, :]
                    copied = q.issue("scalar", lambda e, src=src, d=d: e.activation(d, src, ACT.Copy), after=[turned, *after])
                turn_banks.release(bslot, copied)
                ready.append(copied)
                if c0 + 4 >= len(chunks):
                    temps.release(slot, turned)
            return ready, [lambda c0=c0: turn(c0) for c0 in range(0, len(chunks), 4)]

        class Attention:

            def __init__(self, queries, keys, values, probs, turned, out_q, key_range, chunks, tile, half, key_tile, value_head,
                         add_bias, exp_scale, sink):
                self.q_hi, self.q_lo = queries
                self.k_hi, self.k_lo = keys
                self.values, self.turned, self.out_q = values, turned, out_q
                self.key_range, self.chunks = key_range, chunks
                self.tile, self.half, self.key_tile, self.value_head = tile, half, key_tile, value_head
                self.add_bias, self.exp_scale, self.sink = add_bias, exp_scale, sink
                self.probs_ring = Ring([probs[:, n] for n in range(3)])
                self.turned_ring = Ring([turned[:, n] for n in range(2)])
                self.inputs_ready, self.values_ready, self.out_ready = [], [], []
                self.group, self.block = {}, {}
                self.out_q_read = None

            def place(self, h):
                return 2 * self.tile(h) + self.half(h)

            def by_place(self, stats, i, g):
                first, step = self.place(4 * g), self.place(4 * g + 1) - self.place(4 * g)
                return stats[:, i % 2, first:first + 3 * step + 1:step]

            def score(self, i, g, n):
                h, (start, count) = 4 * g + n, self.key_range[i]
                if n == 0:
                    slot, probs, free = self.probs_ring.take()
                    self.group[i, g] = {"slot": slot, "probs": probs, "free": free}
                state = self.group[i, g]
                rows = slice(HEAD * self.half(h), HEAD * self.half(h) + HEAD)
                cols = slice(i * BLOCK, (i + 1) * BLOCK)
                t, kt = self.tile(h), self.key_tile(h)
                slot, bank, free = score_banks.take()
                q.wait("tensor", *free, *self.inputs_ready)
                pairs = ((self.q_hi, self.k_hi), (self.q_hi, self.k_lo), (self.q_lo, self.k_hi))
                for m, (qs, ks) in enumerate(pairs):
                    done = q.issue("tensor", lambda e, qs=qs, ks=ks, m=m: e.matmul(
                        bank[:, 0:count], qs[rows, t, cols], kt(ks)[rows, start:start + count], start=m == 0, stop=m == 2),
                        signal=m == 2)
                scored = self.add_bias(i, h, bank[:, 0:count], state["probs"][:, n, 0:count], [done, *state["free"]])
                score_banks.release(slot, scored)
                if n == GROUP - 1:
                    self.softmax(i, g, scored)

            def softmax(self, i, g, scored):
                state, count = self.group[i, g], self.key_range[i][1]
                probs, heads = state["probs"], slice(4 * g, 4 * g + 4)
                top, neg, shift = (a[:, i % 2, heads] for a in (row_max, neg_max, sink_shift))
                done = q.issue("vector", lambda e: e.tensor_reduce(top, probs[:, :, 0:count], AX_X, ALU.max),
                               after=[scored, self.block.get(i - 2)])
                if self.sink is not None:
                    done = q.issue("vector", lambda e: e.tensor_tensor(top, top, sinks_8[:, self.sink, heads], ALU.max),
                                   after=[done, sinks8_ready])
                done = q.issue("vector", lambda e: e.tensor_scalar(neg, top, -self.exp_scale, None, ALU.mult), after=[done])
                if self.sink is not None:
                    shifted = q.issue("vector", lambda e: e.tensor_tensor(shift, sinks[:, self.sink, heads], neg, ALU.add),
                                      after=[done])
                for n in range(GROUP):
                    p, s = probs[:, n, 0:count], self.place(4 * g + n)
                    exps = q.issue("scalar", lambda e, p=p, n=n, s=s: e.activation(
                        p, p, ACT.Exp, bias=neg[:, n:n + 1], scale=self.exp_scale, accum_out=row_sum[:, i % 2, s:s + 1]),
                        after=[done, self.block.get(i - 2)])
                if self.sink is not None:
                    exps = q.issue("scalar", lambda e: e.activation(self.by_place(sink_exp, i, g), shift, ACT.Exp),
                                   after=[shifted])
                state["exps"] = exps

            def turn(self, i, g, c):
                state = self.group[i, g]
                value_chunk, offset, rows = self.chunks[i][c]
                bslot, bank, bfree = turn_banks.take()
                q.wait("tensor", state["exps"], identity_in, *bfree)
                for n in range(GROUP):
                    turned = q.issue("tensor", lambda e, n=n: e.transpose(
                        bank[0:rows, n * P:(n + 1) * P], state["probs"][:, n, offset:offset + rows], identity[:, :]),
                        signal=n == 3)
                slot, dst, free = self.turned_ring.take()
                copied = q.issue("scalar", lambda e: e.activation(dst[0:rows, :], bank[0:rows, :], ACT.Copy), after=[turned, *free])
                turn_banks.release(bslot, copied)
                state[c] = (slot, dst, copied)
                if c == len(self.chunks[i]) - 1:
                    self.probs_ring.release(state["slot"], turned)

            def multiply(self, i, g, c):
                slot, turned, copied = self.group[i, g][c]
                value_chunk, _, rows = self.chunks[i][c]
                if g == 0 and c == 0:
                    self.value_slot, self.value_bank, free = value_bank.take()
                    q.wait("tensor", *free)
                bank = self.value_bank
                q.wait("tensor", copied, *self.values_ready)
                last_chunk = c == len(self.chunks[i]) - 1
                for n in range(GROUP):
                    h = 4 * g + n
                    cols = slice(HEAD * self.place(h), HEAD * self.place(h) + HEAD)
                    done = q.issue("tensor", lambda e, n=n, h=h, cols=cols: e.matmul(
                        bank[:, cols], turned[0:rows, n * P:(n + 1) * P], self.values[0:rows, value_chunk, self.value_head(h), :],
                        start=g == 0 and c == 0 and n == 0, stop=last_chunk, skip_group_check=True), signal=n == 3)
                self.turned_ring.release(slot, done)
                if g == 1 and last_chunk:
                    self.normalise(i, done)

            def normalise(self, i, done):
                total, inv, bank = row_sum[:, i % 2, :], row_inv[:, i % 2, :], self.value_bank
                ready = [self.group[i, 0]["exps"], self.group[i, 1]["exps"]]
                if self.sink is not None:
                    ready = [q.issue("vector", lambda e: e.tensor_tensor(total, total, sink_exp[:, i % 2, :], ALU.add), after=ready)]
                inverse = q.issue("vector", lambda e: e.reciprocal(inv, total), after=ready)
                heads = lambda ap: ap.rearrange("p (h d) -> p h d", d=HEAD)
                self.block[i] = q.issue("vector", lambda e: e.tensor_tensor(
                    heads(self.out_q[:, :]), heads(bank[:, :]), inv.unsqueeze(2).broadcast_to([P, HEADS, HEAD]), ALU.mult),
                    after=[inverse, done, self.out_q_read])
                value_bank.release(self.value_slot, self.block[i])

            def turn_out(self, i):
                bslot, bank, bfree = turn_banks.take()
                q.wait("tensor", self.block[i], identity_in, *bfree)
                for t in range(4):
                    turned = q.issue("tensor", lambda e, t=t: e.transpose(
                        bank[:, t * P:(t + 1) * P], self.out_q[:, t * P:(t + 1) * P], identity[:, :]), signal=t == 3)
                self.out_q_read = turned
                cols = slice(i * BLOCK, (i + 1) * BLOCK)
                src = bank[:, :].rearrange("p (t n) -> p t n", t=4)
                hi, lo = self.q_hi[:, :, cols], self.q_lo[:, :, cols]
                hi_done = q.issue("scalar", lambda e: e.activation(hi, src, ACT.Copy), after=[turned])
                lo_done = q.issue("vector", lambda e: e.tensor_tensor(lo, src, hi.bitcast(F32), ALU.subtract), after=[hi_done])
                turn_banks.release(bslot, lo_done)
                self.out_ready += [hi_done, lo_done]

            def steps(self, first, period, delay):
                steps = []
                for i in range(BLOCKS):
                    for g in range(2):
                        at = first + period * (2 * i + g)
                        steps += [(at + n, lambda i=i, g=g, n=n: self.score(i, g, n)) for n in range(GROUP)]
                        chunks = range(len(self.chunks[i]))
                        steps += [(at + delay + 2 * c, lambda i=i, g=g, c=c: self.turn(i, g, c)) for c in chunks]
                        steps += [(at + delay + 3 + 2 * c, lambda i=i, g=g, c=c: self.multiply(i, g, c)) for c in chunks]
                    steps.append((at + delay + 2 * len(chunks) + 5, lambda i=i: self.turn_out(i)))
                return steps

        def alibi(dist, first_offset):
            def add_bias(i, h, scores, dst, after):
                n = scores.shape[1]
                lo = first_offset if i == 0 else 0
                slope = 2.0 ** -(h + 1)
                return q.issue("vector", lambda e: e.scalar_tensor_tensor(dst, dist[:, lo:lo + n], -slope / SCALE, scores, ALU.mult, ALU.add),
                               after=[*after, dist1_in, dist2_in])
            return add_bias

        window_1 = [(max(0, i - 1) * BLOCK, (min(BLOCKS, i + 2) - max(0, i - 1)) * BLOCK) for i in range(BLOCKS)]
        chunks_1 = [[(s // BLOCK + c, c * BLOCK, BLOCK) for c in range(n // BLOCK)] for s, n in window_1]
        window_2 = [(max(0, i - 1) * BLOCK, (i + 1 - max(0, i - 1)) * BLOCK) for i in range(BLOCKS)]
        chunks_2 = [[(s // BLOCK + c, c * BLOCK, BLOCK) for c in range(n // BLOCK)] for s, n in window_2]
        gqa = dict(tile=lambda h: h % GROUP, half=lambda h: h // GROUP, key_tile=lambda h: (lambda k: k),
                   value_head=lambda h: h // GROUP, exp_scale=SCALE)
        half_block = BLOCK // 2
        window_b = [(0, BLOCK + half_block)] + [(i * BLOCK - half_block, 2 * BLOCK) for i in (1, 2)] + \
                   [((BLOCKS - 1) * BLOCK - half_block, BLOCK + half_block)]
        value_chunks_b = [(0, half_block)] + [(j * BLOCK - half_block, BLOCK) for j in range(1, BLOCKS)] + \
                         [(TOKENS - half_block, half_block)]
        chunks_b = []
        for i in range(BLOCKS):
            a, b = value_chunks_b[i], value_chunks_b[i + 1]
            chunks_b.append([(i, 0, a[1]), (i + 1, a[1], b[1])])

        split_unit(0)
        dense_first()

        rel_rows = 8 * HEADS
        rel_in_slot, rel_in, rel_in_free = temps.take()
        for r in range(GRID_R):
            rel_here = q.dma("gpsimd", lambda e, r=r: e.dma_start(
                rel_in[r * HEADS:(r + 1) * HEADS, 0:GRID_R * REL_C].rearrange("h (a b) -> h a b", a=GRID_R),
                dram["rpb"][:, GRID_R - 1 - r:2 * GRID_R - 1 - r, :]), rel_landed, after=rel_in_free if r == 0 else ())
        rel_out_slot, rel_out, rel_out_free = temps.take()
        cleared = q.issue("gpsimd", lambda e: e.memset(rel_out[0:rel_rows, 0:REL_PAD], 0.0), after=rel_out_free)
        pad = 8 * GRID_R
        spread = q.issue("gpsimd", lambda e: e.tensor_copy(
            rel_out[0:rel_rows, pad:pad + REL_C * GRID_R].rearrange("p (d r) -> p d r", r=GRID_R),
            rel_in[0:rel_rows, 0:GRID_R * REL_C].rearrange("p (r d) -> p d r", r=GRID_R)), after=[rel_here, cleared])
        rel_kept = q.dma("sync", lambda e: e.dma_start(dram["rel_scratch"], rel_out[0:rel_rows, 0:REL_PAD]), rel_stored, after=[spread])
        temps.release(rel_in_slot, spread)
        temps.release(rel_out_slot, rel_kept)
        for c in range(BLOCK_C):
            off = (BLOCK_C - 1 - c) * GRID_R
            bias_here = q.dma("gpsimd", lambda e, c=c, off=off: e.dma_start(
                rel_bias[c * GRID_R:(c + 1) * GRID_R, :, :],
                dram["rel_scratch"].rearrange("(r h) x -> r h x", h=HEADS)[:, :, off:off + 2 * BLOCK]),
                bias_landed, after=[rel_kept])

        chunks_v = [(j * BLOCK, BLOCK) for j in range(BLOCKS)]

        def qkv_gqa(q_hi, q_lo, k_hi, k_lo, v, after=(), after_v=6):
            ready = list(project_split(k_hi[:, :], k_lo[:, :], after=after))
            v_ready, turns = project_v(v, (0, 1), chunks_v, after=after)
            start_beside([(after_v + n, turn) for n, turn in enumerate(turns)])
            ready += project_split(q_hi[:, 0, :], q_lo[:, 0, :], after=after)
            for t in range(1, 4):
                ready += project_split(q_hi[:, t, :], q_lo[:, t, :], after=after)
            return ready, v_ready

        attn_a = Attention((qa_hi, qa_lo), (ka_hi, ka_lo), va, probs_1, probs_t1, out_q1, window_1, chunks_1,
                           add_bias=alibi(dist_1, BLOCK), sink=0, **gqa)
        attn_a.inputs_ready, attn_a.values_ready = qkv_gqa(qa_hi, qa_lo, ka_hi, ka_lo, va, after_v=12)

        attn_b = Attention((qb_hi, qb_lo), (kb_hi, kb_lo), vb, probs_1, probs_t1, out_q1, window_b, chunks_b,
                           tile=lambda h: h // 2, half=lambda h: h % 2, key_tile=lambda h: (lambda k: k[:, h // 2, :]),
                           value_head=lambda h: h, add_bias=None, exp_scale=1.0, sink=None)
        attn_b.values_tokens = []
        lo_engine[0] = "gpsimd"
        start_beside(attn_a.steps(first=5, period=10, delay=11))
        for t in range(4):
            ready, turns = project_v(vb, (2 * t, 2 * t + 1), value_chunks_b, view=by_column)
            attn_b.values_tokens.append(ready)
            beside["steps"] = sorted(beside["steps"] + [(beside["slot"] + 6 + 2 * n, turn) for n, turn in enumerate(turns)],
                                     key=lambda s: s[0])
            attn_b.inputs_ready += project_split(kb_hi[:, t, :], kb_lo[:, t, :], view=by_column)
        for t in range(4):
            attn_b.inputs_ready += project_split(qb_hi[:, t, :], qb_lo[:, t, :], view=by_column)
        finish_beside()

        after_a = barrier()
        attn_b.values_ready = [t for ready in attn_b.values_tokens for t in ready]
        attn_b.probs_ring.users = attn_a.probs_ring.users
        attn_b.turned_ring.users = attn_a.turned_ring.users
        attn_b.out_q_read = attn_a.out_q_read
        attn_b.block = {-2: attn_a.block[BLOCKS - 2], -1: attn_a.block[BLOCKS - 1]}
        bias_read, bias_ready = {0: [], 1: []}, {}

        def mask_bias(i, g):
            if i == 2:
                return
            if i == 0:
                first, lower, upper = half_block // GRID_R, (8, 24), (24, 32)
            elif i == 1:
                first, lower, upper = 0, (0, 32), (0, 32)
            else:
                first, lower, upper = 0, (0, 8), (8, 24)
            heads = slice(4 * g, 4 * g + 4)
            view = lambda t, a, b: t[:, heads, :].rearrange("p h (j r) -> p h j r", r=GRID_R)[:, :, a:b, :]
            token = None
            for n, ((a, b), sign, base) in enumerate(((lower, 1, GRID_R - 1), (upper, -1, (WIN_W - 1) * GRID_R))):
                in_place = i == 1 and n == 1
                dst_v = view(masked_bias, a - first, b - first)
                src_v = view(masked_bias, a, b) if in_place else view(rel_bias, a, b)
                token = q.issue("gpsimd", lambda e, dst_v=dst_v, src_v=src_v, a=a, b=b, sign=sign, base=base: e.affine_select(
                    out=dst_v, in_=src_v, compare_op=ALU.is_ge, fill=-MASKED, base=base + sign * GRID_R * a,
                    pattern=[[0, 4], [sign * GRID_R, b - a], [0, GRID_R]], channel_multiplier=-sign),
                    after=[bias_here, *bias_read[g], token])
            bias_ready[g] = token

        def add_rel_bias(i, h, scores, dst, after):
            n = scores.shape[1]
            token = q.issue("vector", lambda e: e.scalar_tensor_tensor(dst, scores, SCALE, masked_bias[:, h, 0:n], ALU.mult, ALU.add),
                            after=[*after, bias_ready[h // 4]])
            bias_read[h // 4] = [token]
            if h % 4 == 3 and i + 1 < BLOCKS:
                mask_bias(i + 1, h // 4)
            return token

        attn_b.add_bias = add_rel_bias

        def act_y(hi, lo):
            return lambda k: (hi[:, k, :], lo[:, k, :])

        merged_ready = [()] * KT
        gate_state = {}

        def gate_job(m, n, bias_col, buffer, after):
            result = dense_h()
            slot, temp, free = temps.take()
            z = scaled(result, temp[:, :], after=free)
            token = q.issue("scalar", lambda e: e.activation(buffer[:, n, :], temp[:, :], ACT.Sigmoid, bias=gate_bias[:, bias_col:bias_col + 1]),
                            after=[z, gate_bias_in, *after, *gate_state.get(n, ())])
            temps.release(slot, token)
            gate_state[n] = (token,)

        def merge_a(m, n):
            slot, bank, done = dense(4, n * P, act_y(qa_hi, qa_lo), lambda k: attn_a.out_ready, last_of_unit=n == 1)
            token = q.issue("vector", lambda e: e.tensor_tensor(x[:, m, :], bank[:, :], gates[:, n, :], ALU.mult),
                            after=[done, *gate_state[n], *barrier_x])
            dense_banks.release(slot, token)
            gate_state[n] = (token,)
            merged_ready[m] = (token,)

        barrier_x = [rms_state["sum"]] + [t for m in range(KT) for t in h_ready[m]]
        mask_bias(0, 0)
        mask_bias(0, 1)
        start_beside(attn_b.steps(first=5, period=10, delay=11))
        for m in range(0, KT, 2):
            for n in range(2):
                gate_job(m + n, n, m + n, gates, after_a)
            for n in range(2):
                merge_a(m + n, n)
        finish_beside()

        after_b = barrier()
        gate_state.clear()

        def merge_b(m, n):
            slot, bank, done = dense(4, n * P, act_y(qb_hi, qb_lo), lambda k: attn_b.out_ready, last_of_unit=n == 1)
            tslot, temp, tfree = temps.take()
            grid = lambda ap: ap.rearrange("p (r c) -> p r c", r=GRID_R)
            part = q.issue("vector", lambda e: e.tensor_tensor(
                grid(temp[:, :]), bank[:, :].rearrange("p (c r) -> p r c", r=GRID_R), grid(gates_b[:, n, :]), ALU.mult),
                after=[done, *gate_state[n], *tfree])
            dense_banks.release(slot, part)
            gate_state[n] = (part,)
            total = q.issue("vector", lambda e: e.tensor_tensor(temp[:, :], temp[:, :], x[:, m, :], ALU.add), after=[part, *merged_ready[m]])
            merged_ready[m] = split_into(temp[:, :], mg_hi[:, m, :], mg_lo[:, m, :], [total])
            temps.release(tslot, *merged_ready[m])
            x_written[m] = (q.dma("gpsimd", lambda e: e.dma_start(x[:, m, :], dram["x"][m * P:(m + 1) * P, :]), x_back[m], after=[total]),)

        lo_engine[0] = "vector"
        for m in range(0, KT, 2):
            for n in range(2):
                gate_job(m + n, n, KT + m + n, gates_b, after_b)
            for n in range(2):
                merge_b(m + n, n)

        def residual(m, result, factor, add_to_norm):
            slot, bank, done = result
            token = q.issue("vector", lambda e: e.scalar_tensor_tensor(x[:, m, :], bank[:, :], factor, x[:, m, :], ALU.mult, ALU.add),
                            after=[done, *x_written[m], *add_to_norm])
            dense_banks.release(slot, token)
            x_written[m] = (token,)

        def out_projection(act, ready, gain, factor=1.0):
            for m in range(KT):
                residual(m, dense(KT, 0, act, ready), factor, ())
                norm_tile(m, gain)

        out_projection(lambda k: (mg_hi[:, k, :], mg_lo[:, k, :]), lambda k: merged_ready[k], 1)

        def mlp(n_tiles, hidden_tile, after, factor, norm):
            ring = Ring(range(ff_ring))
            ring.users = [tuple(after)] * ff_ring
            sizes = [min(FF_CHUNK, n_tiles - s) for s in range(0, n_tiles, FF_CHUNK)]
            held = []

            for c, size in enumerate(sizes):
                if len(held) == c:
                    held.append([])
                while len(held[c]) < size:
                    slot, _, free = ring.take()
                    held[c].append((slot, hidden_tile(act_hi[:, slot, :], act_lo[:, slot, :], free)))
                if c + 1 < len(sizes):
                    slot, _, free = ring.take()
                    held.append([(slot, hidden_tile(act_hi[:, slot, :], act_lo[:, slot, :], free))])
                tiles = held[c]
                for m in range(KT):
                    result = dense(size, 0, lambda k: (act_hi[:, tiles[k][0], :], act_lo[:, tiles[k][0], :]), lambda k: tiles[k][1])
                    residual(m, result, factor, ())
                    if c == len(sizes) - 1:
                        norm(m)
                for slot, _ in tiles:
                    ring.users[slot] = (result[2],)

        def relu_squared(hi, lo, free):
            result = dense_h()
            slot, bank, done = result
            s1, positive, f1 = temps.take()
            token = q.issue("vector", lambda e: e.scalar_tensor_tensor(positive[:, :], bank[:, :], 0.0, rms_inv[:, :], ALU.max, ALU.mult),
                            after=[done, rms_state["ready"], *f1])
            dense_banks.release(slot, token)
            s2, squared, f2 = temps.take()
            square = q.issue("scalar", lambda e: e.activation(squared[:, :], positive[:, :], ACT.Square), after=[token, *f2])
            temps.release(s1, square)
            tokens = split_into(squared[:, :], hi, lo, [square], hi_after=free)
            temps.release(s2, *tokens)
            return tokens

        def swiglu(hi, lo, free):
            gate = dense_h()
            s1, temp, f1 = temps.take()
            g = scaled(gate, temp[:, :], after=f1)
            s2, act, f2 = temps.take()
            silu = q.issue("scalar", lambda e: e.activation(act[:, :], temp[:, :], ACT.Silu), after=[g, *f2])
            temps.release(s1, silu)
            up = dense_h()
            s3, value, f3 = temps.take()
            v = scaled(up, value[:, :], after=f3)
            product = q.issue("vector", lambda e: e.tensor_tensor(value[:, :], value[:, :], act[:, :], ALU.mult), after=[v, silu])
            temps.release(s2, product)
            tokens = split_into(value[:, :], hi, lo, [product], hi_after=free)
            temps.release(s3, *tokens)
            return tokens

        pending_norm[0] = norm_finish
        for_both = q.issue("vector", lambda e: e.tensor_tensor(gain_product[:, :], gains[:, 2, :], gains[:, 3, :], ALU.mult),
                           after=[gains_in])

        def norm_tile_twice(m):
            q.wait("scalar", for_both)
            q.wait("vector", for_both)
            h_tile(m, gain_product[:, m:m + 1])
            square_tile(m)
            square_tile(m, scaled_square_sum, "sum_scaled", gains[:, 2, m:m + 1])

        mlp(FF1_TILES, relu_squared, barrier(), 1.0, norm_tile_twice)

        def final_norm(gain, scale, then):
            for m in range(KT):
                x_written[m] = (q.issue("vector", lambda e, m=m: e.scalar_tensor_tensor(
                    x[:, m, :], x[:, m, :], gains[:, gain, m:m + 1], scale[:, :], ALU.mult, ALU.mult),
                    after=[*x_written[m], *h_ready[m], *scale_ready]),)
                then(m)

        def norm_and_rescale():
            norm_finish_twice()
            scale_ready[:] = [rms_state["first"], rms_state["sum"], rms_state["sum_scaled"]]
            final_norm(2, rms_first, lambda m: None)

        scale_ready = []
        pending_norm[0] = norm_and_rescale

        for layer in range(LAYERS_2):
            base = 3 + 3 * layer
            if layer > 0:
                pending_norm[0] = norm_finish
            mlp(FF2_TILES, swiglu, () if layer == 0 else barrier(), 0.5, lambda m: norm_tile(m, base + 1))
            start = barrier()
            padded = q.issue("vector", lambda e: e.memset(conv_u[:, 0:2], 0.0), after=start)
            attn = Attention((q2_hi, q2_lo), (k2_hi, k2_lo), v2, probs_2, probs_t2, out_q2, window_2, chunks_2,
                             add_bias=alibi(dist_2, BLOCK), sink=1 + layer, **gqa)
            pending_norm[0] = norm_finish
            attn.inputs_ready, attn.values_ready = qkv_gqa(q2_hi, q2_lo, k2_hi, k2_lo, v2, after=start)
            attn.probs_ring.users = [tuple(start)] * 3
            attn.turned_ring.users = [tuple(start)] * 2
            conv = {"c": start, "u": [padded], "y": start}
            cat_ready = []

            def conv_c_job():
                conv["c"] = [scaled(dense_h(), conv_c[:, :], after=conv["c"])]

            def conv_h_job(f, layer=layer):
                slot, temp, free = temps.take()
                hz = scaled(dense_h(), temp[:, :], after=free)
                u = q.issue("gpsimd", lambda e: e.tensor_tensor(conv_u[:, 2:TOKENS + 2], temp[:, :], conv_c[:, :], ALU.mult),
                            after=[hz, *conv["c"], *conv["u"]])
                temps.release(slot, u)
                conv["c"] = [u]
                w = lambda k: conv_w[:, layer, f, k:k + 1]
                y = q.issue("scalar", lambda e: e.activation(conv_y[:, :], conv_u[:, 2:TOKENS + 2], ACT.Copy, scale=w(2)),
                            after=[u, padded, conv_w_in, *conv["y"]])
                for k in (1, 0):
                    y = q.issue("vector", lambda e, k=k: e.scalar_tensor_tensor(
                        conv_y[:, :], conv_u[:, k:k + TOKENS], w(k), conv_y[:, :], ALU.mult, ALU.add), after=[y, u, padded])
                conv["u"] = [y]
                conv["y"] = [y]

            def conv_b_job(f, start=start):
                slot, temp, free = temps.take()
                bz = scaled(dense_h(), temp[:, :], after=free)
                o = q.issue("gpsimd", lambda e: e.tensor_tensor(temp[:, :], temp[:, :], conv_y[:, :], ALU.mult), after=[bz, *conv["y"]])
                conv["y"] = [o]
                tokens = split_into(temp[:, :], cv_hi[:, f, :], cv_lo[:, f, :], [o], hi_after=start)
                temps.release(slot, *tokens)
                cat_ready.append(tokens)

            lo_engine[0] = "gpsimd"
            start_beside(attn.steps(first=5, period=9, delay=11))
            for f in range(4):
                conv_c_job()
                conv_h_job(f)
                conv_b_job(f)
            finish_beside()
            lo_engine[0] = "vector"
            cat = [(cv_hi[:, f, :], cv_lo[:, f, :], cat_ready[f]) for f in range(4)]
            cat[3:3] = [(q2_hi[:, t, :], q2_lo[:, t, :], attn.out_ready) for t in range(4)]
            out_projection(lambda k: cat[k][:2], lambda k: cat[k][2], base + 2)
            pending_norm[0] = norm_finish
            last = layer == LAYERS_2 - 1
            mlp(FF2_TILES, swiglu, barrier(), 0.5, lambda m: norm_tile(m, None if last else base + 3))

        norm_finish()
        stores = []
        scale_ready[:] = [rms_state["ready"], rms_state["sum"]]
        final_norm(9, rms_inv, lambda m: stores.append(q.dma("sync", lambda e: e.dma_start(out[m * P:(m + 1) * P, :], x[:, m, :]),
                                                    out_stored, after=x_written[m])))
        q.wait("sync", stores[-1])
        assert current[0] == len(units)

        block = stack.enter_context(nc.Block())
        for name in engines:
            def program(engine, name=name):
                for instruction in q.todo[name]:
                    instruction(engine)
            in_block = {"tensor": block.tensor, "vector": block.vector, "scalar": block.scalar,
                            "gpsimd": block.gpsimd, "sync": block.sync}[name]
            in_block(program)


def plan_units(dram):
    units = []

    def column_tiles(w, tiles):
        units.extend((w[t].rearrange("p k n -> p (k n)"), w.shape[2] * w.shape[3]) for t in tiles)

    def down(w, chunk, size):
        for m in range(KT):
            src = w[m, :, chunk * FF_CHUNK:chunk * FF_CHUNK + size, :].rearrange("p k n -> p (k n)")
            units.append((src, size * P))

    def mlp(ups, w_down, n_tiles):
        n_chunks = -(-n_tiles // FF_CHUNK)
        done = 0
        for c in range(n_chunks):
            size = min(FF_CHUNK, n_tiles - c * FF_CHUNK)
            until = min(n_tiles, c * FF_CHUNK + size + 1)
            for t in range(done, until):
                for w in ups:
                    column_tiles(w, [t])
            done = until
            down(w_down, c, size)

    column_tiles(dram["w_in"], range(18))
    for pair in range(KT // 2):
        column_tiles(dram["w_in"], [18 + 2 * pair, 19 + 2 * pair])
        column_tiles(dram["w_proj_a"], [pair])
    for pair in range(KT // 2):
        column_tiles(dram["w_in"], [26 + 2 * pair, 27 + 2 * pair])
        column_tiles(dram["w_proj_b"], [pair])
    column_tiles(dram["w_out"], range(KT))
    mlp([dram["w_up"]], dram["w_down"], FF1_TILES)
    for layer in range(LAYERS_2):
        mlp([dram["ffn1_wg"][layer], dram["ffn1_wu"][layer]], dram["ffn1_wd"][layer], FF2_TILES)
        column_tiles(dram["w_in_2"][layer], range(18))
        column_tiles(dram["w_out_2"][layer], range(KT))
        mlp([dram["ffn2_wg"][layer], dram["ffn2_wu"][layer]], dram["ffn2_wd"][layer], FF2_TILES)
    return units



def tiled(w, width=P, columns=None, rows=None):
    if rows is not None:
        w = w[rows]
    if columns is not None:
        w = w[:, columns]
    k, n = w.shape
    return np.ascontiguousarray(w.reshape(k // P, P, n // width, width).transpose(2, 1, 0, 3))


def head_order():
    return np.concatenate([np.arange(HEAD) + HEAD * h for m in range(GROUP) for h in (m, m + GROUP)])


def distances():
    query = np.arange(BLOCK)[:, None]
    both = np.abs(query + BLOCK - np.arange(3 * BLOCK)[None, :])
    past = query + BLOCK - np.arange(2 * BLOCK)[None, :]
    return (np.where(both <= BLOCK, both, MASKED).astype(np.float32),
            np.where((past >= 0) & (past < BLOCK), past, MASKED).astype(np.float32))


def kernel(**inputs):
    import concourse.bacc as bacc
    from concourse.bass_utils import run_bass_kernel_spmd

    a = {name: np.asarray(value) for name, value in inputs.items()}
    order = head_order()
    width = HEADS * HEAD
    kv = KV_HEADS * HEAD
    at = np.arange(a["w_in"].shape[2])
    b0 = width + 2 * kv
    cols_1 = [at[width:width + kv], at[width + kv:b0], order]
    for t in range(4):
        cols_1 += [at[b0 + 2 * width + t * P:b0 + 2 * width + (t + 1) * P], at[b0 + width + t * P:b0 + width + (t + 1) * P]]
    cols_1 += [at[b0:b0 + width], at[b0 + 3 * width:]]
    at2 = np.arange(a["w_in_2"].shape[2])
    cols_2 = [at2[width:width + kv], at2[width + kv:b0], order]
    for f in range(4):
        b, c, h = (b0 + n * width + f * P for n in range(3))
        cols_2 += [at2[c:c + P], at2[h:h + P], at2[b:b + P]]
    cols_1, cols_2 = np.concatenate(cols_1), np.concatenate(cols_2)
    rows_2 = np.concatenate([np.arange(width, 2 * width - P), order, np.arange(2 * width - P, 2 * width)])
    both = lambda f, w: np.stack([f(w[layer]) for layer in range(LAYERS_2)])
    column = lambda g: g.reshape(-1, P).T
    gains = [a["norm_mix"][0], a["norm_mlp"][0], a["norm_final"]]
    for layer in range(LAYERS_2):
        gains += [a[n][layer] for n in ("ffn1_norm_2", "mix_norm_2", "ffn2_norm_2")]
    gains.append(a["final_norm_2"])
    dist_1, dist_2 = distances()
    arrays = {
        "x": a["x"][0].T,
        "gains": np.stack([column(g) for g in gains], axis=1),
        "dist_1": dist_1, "dist_2": dist_2, "identity": np.eye(P, dtype=np.float32),
        "gate_bias": column(a["b_gate"][0]),
        "sinks": np.concatenate([a["sink"], a["attn_sink_2"]]),
        "conv_w": a["conv_w_2"].reshape(LAYERS_2, 3, 4, P).transpose(3, 0, 2, 1),
        "rpb": a["rpb"][0],
        "w_in": tiled(a["w_in"][0], columns=cols_1),
        "w_proj_a": tiled(a["w_proj_a"][0], 2 * P, rows=order),
        "w_proj_b": tiled(a["w_proj_b"][0], 2 * P),
        "w_out": tiled(a["w_out"][0]),
        "w_up": tiled(a["w_up"][0]), "w_down": tiled(a["w_down"][0]),
        "w_in_2": both(lambda w: tiled(w, columns=cols_2), a["w_in_2"]),
        "w_out_2": both(lambda w: tiled(w, rows=rows_2), a["w_out_2"]),
    }
    for n in ("ffn1", "ffn2"):
        for w in ("wg", "wu", "wd"):
            arrays[f"{n}_{w}"] = both(tiled, a[f"{n}_{w}_2"])
    arrays = {name: np.ascontiguousarray(v) for name, v in arrays.items()}

    nc = bacc.Bacc("TRN2", target_bir_lowering=False, num_devices=1)
    dram = {name: nc.dram_tensor(f"{name}_dram", v.shape, mybir.dt.from_np(v.dtype), kind="ExternalInput").ap()
            for name, v in arrays.items()}
    dram["rel_scratch"] = nc.dram_tensor("rel_scratch_dram", (GRID_R * HEADS, REL_PAD), F32, kind="Internal").ap()
    out = nc.dram_tensor("out_dram", (D_MODEL, TOKENS), F32, kind="ExternalOutput").ap()
    two_blocks(nc, dram, out)
    result = run_bass_kernel_spmd(nc, [{f"{name}_dram": v for name, v in arrays.items()}], core_ids=[0])
    return np.ascontiguousarray(result.results[0]["out_dram"].T)[None]
```

```python
from contextlib import ExitStack

import numpy as np
import concourse.bass as bass
from concourse import mybir

F32 = mybir.dt.float32
F32R = mybir.dt.float32r
ALU = mybir.AluOpType
ACT = mybir.ActivationFunctionType
AX_X = mybir.AxisListType.X

P = 128
TOKENS = 512
D_MODEL = 1024
HEAD = 64
HEADS = 8
KV_HEADS = 2
GROUP = HEADS // KV_HEADS
BLOCK = 128
BLOCKS = TOKENS // BLOCK
KT = D_MODEL // P
FF_CHUNK = 8
FF1_TILES = 4096 // P
FF2_TILES = 2816 // P
LAYERS_2 = 2
EPS = 1e-6
EXP_LATER = 2
SPLIT_LATER = 1
SCALE = HEAD ** -0.5
MASKED = 1e30
UNIT = KT * P
GRID_W = 64
GRID_R = TOKENS // GRID_W
WIN_W = 16
BLOCK_C = BLOCK // GRID_R
SPAN_C = 2 * BLOCK_C
REL_R = 15
REL_C = 31
REL_PAD = (BLOCK_C - 1 + SPAN_C) * GRID_R


class Semaphore:

    def __init__(self, handle):
        self.handle, self.value = handle, 0

    def next(self, amount):
        self.value += amount
        return (self, self.value)


class Queues:

    def __init__(self, engines):
        self.todo = {name: [] for name in engines}
        self.seen = {name: {} for name in engines}
        self.done = {}

    def wait(self, engine, *tokens):
        for token in tokens:
            if token is None:
                continue
            semaphore, value = token
            if value <= self.seen[engine].get(semaphore, 0):
                continue
            self.seen[engine][semaphore] = value
            self.todo[engine].append(lambda e, h=semaphore.handle, v=value: e.wait_ge(h, v))

    def issue(self, engine, make, after=(), signal=True):
        self.wait(engine, *after)
        if not signal:
            self.todo[engine].append(make)
            return None
        token = self.done[engine].next(1)
        self.todo[engine].append(lambda e, h=token[0].handle: make(e).then_inc(h, 1))
        return token

    def dma(self, engine, make, semaphore, after=()):
        self.wait(engine, *after)
        token = semaphore.next(16)
        self.todo[engine].append(lambda e, h=semaphore.handle: make(e).then_inc(h, 16))
        return token


class Ring:

    def __init__(self, buffers):
        self.buffers, self.users, self.at = list(buffers), [()] * len(buffers), -1

    def take(self):
        self.at = (self.at + 1) % len(self.buffers)
        free, self.users[self.at] = self.users[self.at], None
        assert free is not None, "still in use"
        return (self, self.at), self.buffers[self.at], free


def release(slot, *tokens):
    ring, at = slot
    ring.users[at] = tokens


def two_blocks(nc, dram, out):
    engines = ("tensor", "vector", "scalar", "gpsimd", "sync")
    q = Queues(engines)
    stack = ExitStack()
    with stack:
        def sbuf(name, shape, dt=F32, on=stack):
            return on.enter_context(nc.sbuf_tensor(name, shape, dt))

        def semaphore(name):
            return Semaphore(stack.enter_context(nc.semaphore(name)))

        x = sbuf("x", [P, KT, TOKENS])
        h_hi = sbuf("h_hi", [P, KT, TOKENS], F32R)
        h_lo = sbuf("h_lo", [P, KT, TOKENS], F32R)
        n_units = 3
        w_raw = [sbuf(f"w_raw{i}", [P, UNIT]) for i in range(n_units)]
        w_hi = [sbuf(f"w_hi{i}", [P, UNIT], F32R) for i in range(n_units)]
        w_lo = [sbuf(f"w_lo{i}", [P, UNIT], F32R) for i in range(n_units)]
        rms_inv = sbuf("rms_inv", [P, TOKENS])
        square_sum = sbuf("square_sum", [P, TOKENS])
        temps = Ring([sbuf(f"temp{i}", [P, TOKENS]) for i in range(5)])
        identity = sbuf("identity", [P, P])
        ones = sbuf("ones", [P, P])
        dist_1 = sbuf("dist_1", [P, 3 * BLOCK])
        dist_2 = sbuf("dist_2", [P, 2 * BLOCK])
        eps_col = sbuf("eps_col", [P, 1])
        gains = sbuf("gains", [P, 10, KT])
        gain_product = sbuf("gain_product", [P, KT])
        gate_bias = sbuf("gate_bias", [P, 2 * KT])
        sinks = sbuf("sinks", [P, 3, HEADS])
        sinks_8 = sbuf("sinks_8", [P, 3, HEADS])
        conv_w = sbuf("conv_w", [P, LAYERS_2, 4, 3])
        row_max = sbuf("row_max", [P, 2, HEADS])
        neg_max = sbuf("neg_max", [P, 2, HEADS])
        sink_shift = sbuf("sink_shift", [P, 2, HEADS])
        sink_exp = sbuf("sink_exp", [P, 2, HEADS])
        row_sum = sbuf("row_sum", [P, 2, HEADS])
        row_inv = sbuf("row_inv", [P, 2, HEADS])

        def phase(tensors, on):
            return [sbuf(n, s, d, on) for n, s, d in tensors]

        ff_phase, mix1, mix2 = ExitStack(), ExitStack(), ExitStack()
        ff_ring = FF_CHUNK + 2
        with ff_phase:
            act_hi, act_lo = phase([("act_hi", [P, ff_ring, TOKENS], F32R), ("act_lo", [P, ff_ring, TOKENS], F32R)], ff_phase)
            scaled_square_sum, rms_first = phase([("scaled_square_sum", [P, TOKENS], F32), ("rms_first", [P, TOKENS], F32)], ff_phase)
        with mix1:
            qa_hi, qa_lo = phase([("qa_hi", [P, 4, TOKENS], F32R), ("qa_lo", [P, 4, TOKENS], F32R)], mix1)
            qb_hi, qb_lo = phase([("qb_hi", [P, 4, TOKENS], F32R), ("qb_lo", [P, 4, TOKENS], F32R)], mix1)
            probs_t1, out_q1, probs_1 = phase([
                ("probs_t1", [P, 2, TOKENS], F32), ("out_q1", [P, TOKENS], F32),
                ("probs_1", [P, 3, GROUP, 3 * BLOCK], F32)], mix1)
            with ExitStack() as kv_part:
                kb_hi, kb_lo = phase([("kb_hi", [P, 4, TOKENS], F32R), ("kb_lo", [P, 4, TOKENS], F32R)], kv_part)
                (vb,) = phase([("vb", [P, BLOCKS + 1, HEADS, HEAD], F32)], kv_part)
                rel_bias, masked_bias = phase([("rel_bias", [P, HEADS, 2 * BLOCK], F32),
                                               ("masked_bias", [P, HEADS, 2 * BLOCK], F32)], kv_part)
                with ExitStack() as part_a:
                    ka_hi, ka_lo, va = phase([("ka_hi", [P, TOKENS], F32R), ("ka_lo", [P, TOKENS], F32R),
                                              ("va", [P, BLOCKS, KV_HEADS, HEAD], F32)], part_a)
                with ExitStack() as part_b:
                    (gates,) = phase([("gates", [P, 2, TOKENS], F32)], part_b)
            with ExitStack() as part_m:
                mg_hi, mg_lo, gates_b = phase([("mg_hi", [P, KT, TOKENS], F32R), ("mg_lo", [P, KT, TOKENS], F32R),
                                               ("gates_b", [P, 2, TOKENS], F32)], part_m)
        with mix2:
            q2_hi, q2_lo = phase([("q2_hi", [P, 4, TOKENS], F32R), ("q2_lo", [P, 4, TOKENS], F32R)], mix2)
            k2_hi, k2_lo, v2 = phase([("k2_hi", [P, TOKENS], F32R), ("k2_lo", [P, TOKENS], F32R),
                                      ("v2", [P, BLOCKS, KV_HEADS, HEAD], F32)], mix2)
            probs_t2, out_q2, probs_2 = phase([
                ("probs_t2", [P, 2, TOKENS], F32), ("out_q2", [P, TOKENS], F32),
                ("probs_2", [P, 3, GROUP, 2 * BLOCK], F32)], mix2)
            cv_hi, cv_lo = phase([("cv_hi", [P, 4, TOKENS], F32R), ("cv_lo", [P, 4, TOKENS], F32R)], mix2)
            conv_c, conv_u, conv_y = phase([("conv_c", [P, TOKENS], F32), ("conv_u", [P, TOKENS + 2], F32),
                                            ("conv_y", [P, TOKENS], F32)], mix2)

        psum = [stack.enter_context(nc.psum_tensor(f"bank{i}", [P, TOKENS], F32)) for i in range(8)]
        dense_banks, score_banks, turn_banks = Ring(psum[0:3]), Ring(psum[3:5]), Ring(psum[5:7])
        value_bank = Ring(psum[7:8])

        for name in engines[:4]:
            q.done[name] = semaphore(f"{name}_done")
        landed = [semaphore(f"weights_landed{i}") for i in range(n_units)]
        consts_landed = [semaphore(f"consts_landed{i}") for i in range(8)]
        x_landed = [semaphore(f"x_landed{i}") for i in range(KT)]
        x_back = [semaphore(f"x_back{i}") for i in range(KT)]
        rel_landed = semaphore("rel_landed")
        rel_stored = semaphore("rel_stored")
        bias_landed = semaphore("bias_landed")
        out_stored = semaphore("out_stored")

        def barrier():
            return [(s, s.value) for s in q.done.values() if s.value]

        def load_const(i, dst, src):
            return q.dma("sync", lambda e: e.dma_start(dst, src), consts_landed[i])

        ones_ready = q.issue("vector", lambda e: e.memset(ones[:, :], 1.0))
        eps_ready = q.issue("vector", lambda e: e.memset(eps_col[:, :], EPS))

        unit_lo_ready = []
        raw_free = [()] * n_units
        split_free = [()] * n_units
        units = plan_units(dram)
        lo_engine = ["vector"]

        fetched = {}

        def fetch_unit(u):
            if u in fetched:
                return fetched[u]
            s, (src, width) = u % n_units, units[u]
            fetched[u] = q.dma("sync", lambda e: e.dma_start(w_raw[s][:, 0:width], src), landed[s], after=raw_free[s])
            return fetched[u]

        gains_in = load_const(0, gains[:, :, :], dram["gains"])
        x_ready = []
        for m in range(KT):
            x_ready.append(q.dma("sync", lambda e, m=m: e.dma_start(x[:, m, :], dram["x"][m * P:(m + 1) * P, :]), x_landed[m]))
            if m < n_units:
                fetch_unit(m)
        identity_in = load_const(3, identity[:, :], dram["identity"])
        dist1_in = load_const(1, dist_1[:, :], dram["dist_1"])
        dist2_in = load_const(2, dist_2[:, :], dram["dist_2"])
        sinks_in = load_const(5, sinks[:, :, :], dram["sinks"].partition_broadcast(P))
        gate_bias_in = load_const(4, gate_bias[:, :], dram["gate_bias"])
        conv_w_in = load_const(6, conv_w[:, :, :, :], dram["conv_w"])

        def split_unit(u):
            s, width = u % n_units, units[u][1]
            raw_here = fetch_unit(u)
            hi = q.issue("scalar", lambda e: e.activation(w_hi[s][:, 0:width], w_raw[s][:, 0:width], ACT.Copy),
                         after=[raw_here, *split_free[s]])
            lo = q.issue(lo_engine[0], lambda e: e.tensor_tensor(w_lo[s][:, 0:width], w_raw[s][:, 0:width],
                                                                 w_hi[s][:, 0:width].bitcast(F32), ALU.subtract),
                         after=[hi, raw_here, *split_free[s]])
            raw_free[s] = (hi, lo)
            unit_lo_ready.append((hi, lo))

        current = [0]
        first_results = []
        beside = {"slot": 0, "steps": []}

        def start_beside(steps):
            beside["steps"] = sorted(beside["steps"] + [(beside["slot"] + at, step) for at, step in steps], key=lambda s: s[0])

        def later(slots, step):
            start_beside([(slots, step)])

        def next_slot():
            while beside["steps"] and beside["steps"][0][0] <= beside["slot"]:
                beside["steps"].pop(0)[1]()
            beside["slot"] += 1

        def finish_beside():
            while beside["steps"]:
                beside["steps"].pop(0)[1]()

        def dense(k_tiles, columns, act, ready, last_of_unit=True, banks=dense_banks):
            u = current[0]
            slot, bank, bank_free = banks.take()
            q.wait("tensor", *unit_lo_ready[u], *bank_free)
            for k in range(k_tiles):
                q.wait("tensor", *ready(k))
                token = k_step(u, bank, k, k_tiles, columns, act)
                if k < k_tiles - 1:
                    next_slot()
            if last_of_unit:
                next_unit(token)
            next_slot()
            return slot, bank, token

        def dense_pair(k_tiles, act, ready):
            u, taken, done = current[0], [dense_banks.take() for _ in range(2)], []
            for ks in (range(k_tiles - 1), (k_tiles - 1,)):
                for n, (_, bank, bank_free) in enumerate(taken):
                    q.wait("tensor", *unit_lo_ready[u + n], *bank_free)
                    for k in ks:
                        q.wait("tensor", *ready(k))
                        token = k_step(u + n, bank, k, k_tiles, 0, act)
                        next_slot()
                    done.append(token)
            results = [(slot, bank, token) for (slot, bank, _), token in zip(taken, done[2:])]
            for _, _, token in results:
                next_unit(token)
            return results

        def k_step(u, bank, k, k_tiles, columns, act):
            s, width = u % n_units, units[u][1] // k_tiles
            hi, lo = act(k)
            lhs = slice(k * width + columns, k * width + columns + P)
            for n, (w, a) in enumerate(((w_hi[s], hi), (w_hi[s], lo), (w_lo[s], hi))):
                first, last = k == 0 and n == 0, k == k_tiles - 1 and n == 2
                token = q.issue("tensor", lambda e, w=w, a=a, first=first, last=last: e.matmul(
                    bank[:, :], w[:, lhs], a, start=first, stop=last), signal=last)
            return token

        def next_unit(token):
            u = current[0]
            split_free[u % n_units] = (token,)
            current[0] += 1
            if u + n_units < len(units):
                fetch_unit(u + n_units)
                later(SPLIT_LATER, lambda: split_unit(u + n_units))

        def dense_first():
            results = [dense_banks.take() for _ in range(n_units)]
            for k in range(KT):
                h_tile(k, gains[:, 0, k:k + 1])
                if k < n_units:
                    split_unit(k)
                if k >= 2:
                    square_tile(k - 2)
            for k in (KT - 2, KT - 1):
                square_tile(k)

            def steps(u, ks):
                q.wait("tensor", *unit_lo_ready[u])
                for k in ks:
                    q.wait("tensor", *h_ready[k])
                    token = k_step(u, results[u][1], k, KT, 0, act_h)
                return token

            side_by_side = KT // 2
            for k in range(side_by_side):
                for u in range(n_units):
                    steps(u, [k])
            for u in range(n_units):
                if u == n_units - 1:
                    norm_finish()
                token = steps(u, range(side_by_side, KT))
                first_results.append((*results[u][:2], token))
                next_unit(token)
                next_slot()
                next_slot()
            first_results.append(dense(KT, 0, act_h, lambda k: h_ready[k], banks=score_banks))
            h_read[0] = (first_results[-1][2],)

        def act_h(k):
            return h_hi[:, k, :], h_lo[:, k, :]

        h_ready = [()] * KT
        h_read = [()]
        x_written = [(t,) for t in x_ready]
        rms_state = {"ready": None, "sum": None, "sum_scaled": None}

        pending_norm = [None]

        def dense_h():
            if first_results:
                return first_results.pop(0)
            result = dense(KT, 0, act_h, lambda k: h_ready[k])
            h_read[0] = (result[2],)
            if pending_norm[0]:
                pending_norm[0]()
                pending_norm[0] = None
            return result

        def split_into(value, hi, lo, after, hi_after=(), lo_engine="vector"):
            hi_done = q.issue("scalar", lambda e: e.activation(hi, value, ACT.Copy), after=[*after, *hi_after])
            lo_done = q.issue(lo_engine, lambda e: e.tensor_tensor(lo, value, hi.bitcast(F32), ALU.subtract),
                              after=[hi_done, *after, *hi_after])
            return hi_done, lo_done

        def h_tile(m, gain_column):
            g = gain_column
            after = [*x_written[m], gains_in]
            hi = q.issue("scalar", lambda e: e.activation(h_hi[:, m, :], x[:, m, :], ACT.Copy, scale=g), after=[*after, *h_read[0]])
            lo = q.issue("vector", lambda e: e.scalar_tensor_tensor(h_lo[:, m, :], x[:, m, :], g, h_hi[:, m, :].bitcast(F32),
                                                                    ALU.mult, ALU.subtract), after=[hi, *after, *h_read[0]])
            h_ready[m] = (hi, lo)

        def square_tile(m, into=square_sum, state="sum", scale=1.0, engine="gpsimd"):
            if m == 0:
                rms_state[state] = q.issue("scalar", lambda e: e.activation(into[:, :], x[:, m, :], ACT.Square, scale=scale),
                                           after=[*x_written[m], rms_state[state]])
                return
            slot, temp, free = temps.take()
            squared = q.issue("scalar", lambda e: e.activation(temp[:, :], x[:, m, :], ACT.Square, scale=scale),
                              after=[*x_written[m], *free])
            rms_state[state] = q.issue(engine, lambda e: e.tensor_tensor(into[:, :], into[:, :], temp[:, :], ALU.add),
                                       after=[squared, rms_state[state]])
            release(slot, rms_state[state])

        def norm_tile(m, gain):
            if gain is not None:
                h_tile(m, gains[:, gain, m:m + 1])
            square_tile(m)

        def sum_partitions(ring, state="sum", source=square_sum):
            slot, bank, free = ring.take()
            summed = q.issue("tensor", lambda e: e.matmul(bank[:, :], ones[:, :], source[:, :], start=True, stop=True),
                             after=[rms_state[state], ones_ready, *free])
            rms_state[state] = summed
            return slot, bank, summed

        def inverse_root(dst, value, scale, bias, after, before=()):
            tslot, temp, tfree = temps.take()
            root = q.issue("scalar", lambda e: e.activation(temp[:, :], value, ACT.Sqrt, bias=bias, scale=scale),
                           after=[*after, eps_ready, *tfree])
            done = q.issue("vector", lambda e: e.reciprocal(dst[:, :], temp[:, :]), after=[root, *before])
            release(tslot, done)
            return root, done

        def norm_finish():
            slot, bank, summed = sum_partitions(value_bank)
            root, rms_state["ready"] = inverse_root(rms_inv, bank[:, :], 1 / D_MODEL, eps_col[:, :], [summed], [rms_state["ready"]])
            release(slot, root)

        def norm_finish_twice():
            slot1, bank1, summed1 = sum_partitions(value_bank)
            slot2, bank2, summed2 = sum_partitions(turn_banks, "sum_scaled", scaled_square_sum)
            tslot, temp, tfree = temps.take()
            part = q.issue("vector", lambda e: e.tensor_scalar(temp[:, :], bank1[:, :], EPS / D_MODEL, EPS * EPS, ALU.mult, ALU.add),
                           after=[summed1, *tfree])
            value = q.issue("vector", lambda e: e.scalar_tensor_tensor(temp[:, :], bank2[:, :], 1 / D_MODEL, temp[:, :], ALU.mult, ALU.add),
                            after=[summed2, part])
            root, rms_state["ready"] = inverse_root(rms_inv, temp[:, :], 1.0, 0.0, [value], [rms_state["ready"]])
            first_root, rms_state["first"] = inverse_root(rms_first, bank1[:, :], 1 / D_MODEL, eps_col[:, :], [summed1, part])
            release(slot1, first_root)
            release(slot2, value)
            release(tslot, root)

        def scaled(result, dst, view=None, after=()):
            slot, bank, done = result
            src, scale = bank[:, :], rms_inv[:, :]
            if view is not None:
                src, scale, dst = view(src), view(scale), dst.rearrange("p (c r) -> p c r", r=GRID_R)
            token = q.issue("vector", lambda e: e.tensor_tensor(dst, src, scale, ALU.mult),
                            after=[done, rms_state["ready"], *after])
            release(slot, token)
            return token

        def by_column(ap):
            return ap.rearrange("p (r c) -> p c r", r=GRID_R)

        def split_later(slot, value, hi, lo, ready, after):
            hi_done = q.issue("scalar", lambda e: e.activation(hi, value, ACT.Copy), after=after)

            def rest():
                lo_done = q.issue("vector", lambda e: e.tensor_tensor(lo, value, hi.bitcast(F32), ALU.subtract), after=[hi_done, *after])
                ready.extend([hi_done, lo_done])
                release(slot, hi_done, lo_done)
            later(2, rest)

        def project_split(hi, lo, ready, view=None, after=()):
            result = dense_h()
            slot, temp, free = temps.take()
            z = scaled(result, temp[:, :], view, after=free)
            split_later(slot, temp[:, :], hi, lo, ready, [z, *after])

        def project_v(dst, heads, chunks, view=None, after=()):
            result = dense_h()
            slot, temp, free = temps.take()
            z = scaled(result, temp[:, :], view, after=free)
            ready = []

            def turn(c0):
                part = chunks[c0:c0 + 4]
                bslot, bank, bfree = turn_banks.take()
                q.wait("tensor", z, identity_in, *bfree)
                for n, (start, rows) in enumerate(part):
                    turned = q.issue("tensor", lambda e, n=n, start=start, rows=rows: e.transpose(
                        bank[0:rows, n * P:(n + 1) * P], temp[:, start:start + rows], identity[:, :]),
                        signal=n == len(part) - 1)
                runs = []
                for n, (_, rows) in enumerate(part):
                    if runs and runs[-1][2] == rows:
                        runs[-1][1] = n + 1
                    else:
                        runs.append([n, n + 1, rows])
                for a, b, rows in runs:
                    src = bank[0:rows, a * P:b * P].rearrange("p (c h d) -> p c h d", c=b - a, h=2)
                    d = dst[0:rows, c0 + a:c0 + b, heads[0]:heads[0] + 2, :]
                    copied = q.issue("scalar", lambda e, src=src, d=d: e.activation(d, src, ACT.Copy), after=[turned, *after])
                release(bslot, copied)
                ready.append(copied)
                if c0 + 4 >= len(chunks):
                    release(slot, turned)
            return ready, [lambda c0=c0: turn(c0) for c0 in range(0, len(chunks), 4)]

        class Attention:

            def __init__(self, queries, keys, values, probs, turned, out_q, key_range, chunks, tile, half, key_tile, value_head,
                         add_bias, exp_scale, sink):
                self.q_hi, self.q_lo = queries
                self.k_hi, self.k_lo = keys
                self.values, self.turned, self.out_q = values, turned, out_q
                self.key_range, self.chunks = key_range, chunks
                self.tile, self.half, self.key_tile, self.value_head = tile, half, key_tile, value_head
                self.add_bias, self.exp_scale, self.sink = add_bias, exp_scale, sink
                self.probs_ring = Ring([probs[:, n] for n in range(3)])
                self.turned_ring = Ring([turned[:, n] for n in range(2)])
                self.inputs_ready, self.values_ready, self.out_ready = [], [], []
                self.group, self.block = {}, {}
                self.out_q_read = None

            def place(self, h):
                return 2 * self.tile(h) + self.half(h)

            def by_place(self, stats, i, g):
                first, step = self.place(4 * g), self.place(4 * g + 1) - self.place(4 * g)
                return stats[:, i % 2, first:first + 3 * step + 1:step]

            def score(self, i, g, n):
                h, (start, count) = 4 * g + n, self.key_range[i]
                if n == 0:
                    slot, probs, free = self.probs_ring.take()
                    self.group[i, g] = {"slot": slot, "probs": probs, "free": free}
                state = self.group[i, g]
                rows = slice(HEAD * self.half(h), HEAD * self.half(h) + HEAD)
                cols = slice(i * BLOCK, (i + 1) * BLOCK)
                t, kt = self.tile(h), self.key_tile(h)
                slot, bank, free = score_banks.take()
                q.wait("tensor", *free, *self.inputs_ready)
                pairs = ((self.q_hi, self.k_hi), (self.q_hi, self.k_lo), (self.q_lo, self.k_hi))
                for m, (qs, ks) in enumerate(pairs):
                    done = q.issue("tensor", lambda e, qs=qs, ks=ks, m=m: e.matmul(
                        bank[:, 0:count], qs[rows, t, cols], kt(ks)[rows, start:start + count], start=m == 0, stop=m == 2),
                        signal=m == 2)
                scored = self.add_bias(i, h, bank[:, 0:count], state["probs"][:, n, 0:count], [done, *state["free"]])
                release(slot, scored)
                if n == GROUP - 1:
                    self.softmax(i, g, scored)

            def softmax(self, i, g, scored):
                state, count = self.group[i, g], self.key_range[i][1]
                probs, heads = state["probs"], slice(4 * g, 4 * g + 4)
                top, neg, shift = (a[:, i % 2, heads] for a in (row_max, neg_max, sink_shift))
                done = q.issue("vector", lambda e: e.tensor_reduce(top, probs[:, :, 0:count], AX_X, ALU.max),
                               after=[scored, self.block.get(i - 2)])
                if self.sink is not None:
                    done = q.issue("vector", lambda e: e.tensor_tensor(top, top, sinks_8[:, self.sink, heads], ALU.max),
                                   after=[done, sinks8_ready])
                done = q.issue("vector", lambda e: e.tensor_scalar(neg, top, -self.exp_scale, None, ALU.mult), after=[done])
                if self.sink is not None:
                    shifted = q.issue("vector", lambda e: e.tensor_tensor(shift, sinks[:, self.sink, heads], neg, ALU.add),
                                      after=[done])

                def exponentials():
                    for n in range(GROUP):
                        p, s = probs[:, n, 0:count], self.place(4 * g + n)
                        exps = q.issue("scalar", lambda e, p=p, n=n, s=s: e.activation(
                            p, p, ACT.Exp, bias=neg[:, n:n + 1], scale=self.exp_scale, accum_out=row_sum[:, i % 2, s:s + 1]),
                            after=[done, self.block.get(i - 2)])
                    if self.sink is not None:
                        exps = q.issue("scalar", lambda e: e.activation(self.by_place(sink_exp, i, g), shift, ACT.Exp),
                                       after=[shifted])
                    state["exps"] = exps
                later(EXP_LATER, exponentials)

            def turn(self, i, g, c):
                state = self.group[i, g]
                value_chunk, offset, rows = self.chunks[i][c]
                bslot, bank, bfree = turn_banks.take()
                q.wait("tensor", state["exps"], identity_in, *bfree)
                for n in range(GROUP):
                    turned = q.issue("tensor", lambda e, n=n: e.transpose(
                        bank[0:rows, n * P:(n + 1) * P], state["probs"][:, n, offset:offset + rows], identity[:, :]),
                        signal=n == 3)
                slot, dst, free = self.turned_ring.take()
                copied = q.issue("scalar", lambda e: e.activation(dst[0:rows, :], bank[0:rows, :], ACT.Copy), after=[turned, *free])
                release(bslot, copied)
                state[c] = (slot, dst, copied)
                if c == len(self.chunks[i]) - 1:
                    release(state["slot"], turned)

            def multiply(self, i, g, c):
                slot, turned, copied = self.group[i, g][c]
                value_chunk, _, rows = self.chunks[i][c]
                if g == 0 and c == 0:
                    self.value_slot, self.value_bank, free = value_bank.take()
                    q.wait("tensor", *free)
                bank = self.value_bank
                q.wait("tensor", copied, *self.values_ready)
                last_chunk = c == len(self.chunks[i]) - 1
                for n in range(GROUP):
                    h = 4 * g + n
                    cols = slice(HEAD * self.place(h), HEAD * self.place(h) + HEAD)
                    done = q.issue("tensor", lambda e, n=n, h=h, cols=cols: e.matmul(
                        bank[:, cols], turned[0:rows, n * P:(n + 1) * P], self.values[0:rows, value_chunk, self.value_head(h), :],
                        start=g == 0 and c == 0 and n == 0, stop=last_chunk, skip_group_check=True), signal=n == 3)
                release(slot, done)
                if g == 1 and last_chunk:
                    self.normalise(i, done)

            def normalise(self, i, done):
                total, inv, bank = row_sum[:, i % 2, :], row_inv[:, i % 2, :], self.value_bank
                ready = [self.group[i, 0]["exps"], self.group[i, 1]["exps"]]
                if self.sink is not None:
                    ready = [q.issue("vector", lambda e: e.tensor_tensor(total, total, sink_exp[:, i % 2, :], ALU.add), after=ready)]
                inverse = q.issue("vector", lambda e: e.reciprocal(inv, total), after=ready)
                heads = lambda ap: ap.rearrange("p (h d) -> p h d", d=HEAD)
                self.block[i] = q.issue("vector", lambda e: e.tensor_tensor(
                    heads(self.out_q[:, :]), heads(bank[:, :]), inv.unsqueeze(2).broadcast_to([P, HEADS, HEAD]), ALU.mult),
                    after=[inverse, done, self.out_q_read])
                release(self.value_slot, self.block[i])

            def turn_out(self, i):
                bslot, bank, bfree = turn_banks.take()
                q.wait("tensor", self.block[i], identity_in, *bfree)
                for t in range(4):
                    turned = q.issue("tensor", lambda e, t=t: e.transpose(
                        bank[:, t * P:(t + 1) * P], self.out_q[:, t * P:(t + 1) * P], identity[:, :]), signal=t == 3)
                self.out_q_read = turned
                cols = slice(i * BLOCK, (i + 1) * BLOCK)
                src = bank[:, :].rearrange("p (t n) -> p t n", t=4)
                hi, lo = self.q_hi[:, :, cols], self.q_lo[:, :, cols]
                hi_done = q.issue("scalar", lambda e: e.activation(hi, src, ACT.Copy), after=[turned])

                def rest():
                    lo_done = q.issue("vector", lambda e: e.tensor_tensor(lo, src, hi.bitcast(F32), ALU.subtract), after=[hi_done])
                    release(bslot, lo_done)
                    self.out_ready += [hi_done, lo_done]
                later(1, rest)

            def steps(self, first, period, delay):
                steps = []
                for i in range(BLOCKS):
                    for g in range(2):
                        at = first + period * (2 * i + g)
                        steps += [(at + n, lambda i=i, g=g, n=n: self.score(i, g, n)) for n in range(GROUP)]
                        chunks = range(len(self.chunks[i]))
                        steps += [(at + delay + 2 * c, lambda i=i, g=g, c=c: self.turn(i, g, c)) for c in chunks]
                        steps += [(at + delay + 3 + 2 * c, lambda i=i, g=g, c=c: self.multiply(i, g, c)) for c in chunks]
                    steps.append((at + delay + 2 * len(chunks) + 5, lambda i=i: self.turn_out(i)))
                return steps

        def alibi(dist, first_offset):
            def add_bias(i, h, scores, dst, after):
                n = scores.shape[1]
                lo = first_offset if i == 0 else 0
                slope = 2.0 ** -(h + 1)
                return q.issue("vector", lambda e: e.scalar_tensor_tensor(dst, dist[:, lo:lo + n], -slope / SCALE, scores, ALU.mult, ALU.add),
                               after=[*after, dist1_in, dist2_in])
            return add_bias

        window_1 = [(max(0, i - 1) * BLOCK, (min(BLOCKS, i + 2) - max(0, i - 1)) * BLOCK) for i in range(BLOCKS)]
        chunks_1 = [[(s // BLOCK + c, c * BLOCK, BLOCK) for c in range(n // BLOCK)] for s, n in window_1]
        window_2 = [(max(0, i - 1) * BLOCK, (i + 1 - max(0, i - 1)) * BLOCK) for i in range(BLOCKS)]
        chunks_2 = [[(s // BLOCK + c, c * BLOCK, BLOCK) for c in range(n // BLOCK)] for s, n in window_2]
        gqa = dict(tile=lambda h: h % GROUP, half=lambda h: h // GROUP, key_tile=lambda h: (lambda k: k),
                   value_head=lambda h: h // GROUP, exp_scale=SCALE)
        half_block = BLOCK // 2
        window_b = [(0, BLOCK + half_block)] + [(i * BLOCK - half_block, 2 * BLOCK) for i in (1, 2)] + \
                   [((BLOCKS - 1) * BLOCK - half_block, BLOCK + half_block)]
        value_chunks_b = [(0, half_block)] + [(j * BLOCK - half_block, BLOCK) for j in range(1, BLOCKS)] + \
                         [(TOKENS - half_block, half_block)]
        chunks_b = []
        for i in range(BLOCKS):
            a, b = value_chunks_b[i], value_chunks_b[i + 1]
            chunks_b.append([(i, 0, a[1]), (i + 1, a[1], b[1])])

        dense_first()
        sinks8_ready = q.issue("vector", lambda e: e.tensor_scalar(sinks_8[:, :, :], sinks[:, :, :], 1 / SCALE, None, ALU.mult),
                               after=[sinks_in])

        rel_rows = 8 * HEADS
        rel_in_slot, rel_in, rel_in_free = temps.take()
        for r in range(GRID_R):
            rel_here = q.dma("gpsimd", lambda e, r=r: e.dma_start(
                rel_in[r * HEADS:(r + 1) * HEADS, 0:GRID_R * REL_C].rearrange("h (a b) -> h a b", a=GRID_R),
                dram["rpb"][:, GRID_R - 1 - r:2 * GRID_R - 1 - r, :]), rel_landed, after=rel_in_free if r == 0 else ())
        rel_out_slot, rel_out, rel_out_free = temps.take()
        cleared = q.issue("gpsimd", lambda e: e.memset(rel_out[0:rel_rows, 0:REL_PAD], 0.0), after=rel_out_free)
        pad = 8 * GRID_R
        spread = q.issue("gpsimd", lambda e: e.tensor_copy(
            rel_out[0:rel_rows, pad:pad + REL_C * GRID_R].rearrange("p (d r) -> p d r", r=GRID_R),
            rel_in[0:rel_rows, 0:GRID_R * REL_C].rearrange("p (r d) -> p d r", r=GRID_R)), after=[rel_here, cleared])
        rel_kept = q.dma("sync", lambda e: e.dma_start(dram["rel_scratch"], rel_out[0:rel_rows, 0:REL_PAD]), rel_stored, after=[spread])
        release(rel_in_slot, spread)
        release(rel_out_slot, rel_kept)
        for c in range(BLOCK_C):
            off = (BLOCK_C - 1 - c) * GRID_R
            bias_here = q.dma("gpsimd", lambda e, c=c, off=off: e.dma_start(
                rel_bias[c * GRID_R:(c + 1) * GRID_R, :, :],
                dram["rel_scratch"].rearrange("(r h) x -> r h x", h=HEADS)[:, :, off:off + 2 * BLOCK]),
                bias_landed, after=[rel_kept])

        chunks_v = [(j * BLOCK, BLOCK) for j in range(BLOCKS)]

        def qkv_gqa(q_hi, q_lo, k_hi, k_lo, v, after=(), after_v=6):
            ready = []
            project_split(k_hi[:, :], k_lo[:, :], ready, after=after)
            v_ready, turns = project_v(v, (0, 1), chunks_v, after=after)
            start_beside([(after_v + n, turn) for n, turn in enumerate(turns)])
            for t in range(4):
                project_split(q_hi[:, t, :], q_lo[:, t, :], ready, after=after)
            return ready, v_ready

        attn_a = Attention((qa_hi, qa_lo), (ka_hi, ka_lo), va, probs_1, probs_t1, out_q1, window_1, chunks_1,
                           add_bias=alibi(dist_1, BLOCK), sink=0, **gqa)
        attn_a.inputs_ready, attn_a.values_ready = qkv_gqa(qa_hi, qa_lo, ka_hi, ka_lo, va, after_v=1)

        attn_b = Attention((qb_hi, qb_lo), (kb_hi, kb_lo), vb, probs_1, probs_t1, out_q1, window_b, chunks_b,
                           tile=lambda h: h // 2, half=lambda h: h % 2, key_tile=lambda h: (lambda k: k[:, h // 2, :]),
                           value_head=lambda h: h, add_bias=None, exp_scale=1.0, sink=None)
        attn_b.values_tokens = []
        lo_engine[0] = "gpsimd"
        start_beside(attn_a.steps(first=5, period=10, delay=11 ))
        for t in range(4):
            ready, turns = project_v(vb, (2 * t, 2 * t + 1), value_chunks_b, view=by_column)
            attn_b.values_tokens.append(ready)
            start_beside([(6 + 2 * n, turn) for n, turn in enumerate(turns)])
            project_split(kb_hi[:, t, :], kb_lo[:, t, :], attn_b.inputs_ready, view=by_column)
        for t in range(4):
            project_split(qb_hi[:, t, :], qb_lo[:, t, :], attn_b.inputs_ready, view=by_column)
        finish_beside()

        after_a = barrier()
        attn_b.values_ready = [t for ready in attn_b.values_tokens for t in ready]
        attn_b.probs_ring.users = attn_a.probs_ring.users
        attn_b.turned_ring.users = attn_a.turned_ring.users
        attn_b.out_q_read = attn_a.out_q_read
        attn_b.block = {-2: attn_a.block[BLOCKS - 2], -1: attn_a.block[BLOCKS - 1]}
        bias_read, bias_ready = {0: [], 1: []}, {}

        def mask_bias(i, g):
            if i == 2:
                return
            if i == 0:
                first, lower, upper = half_block // GRID_R, (8, 24), (24, 32)
            elif i == 1:
                first, lower, upper = 0, (0, 32), (0, 32)
            else:
                first, lower, upper = 0, (0, 8), (8, 24)
            heads = slice(4 * g, 4 * g + 4)
            view = lambda t, a, b: t[:, heads, :].rearrange("p h (j r) -> p h j r", r=GRID_R)[:, :, a:b, :]
            token = None
            for n, ((a, b), sign, base) in enumerate(((lower, 1, GRID_R - 1), (upper, -1, (WIN_W - 1) * GRID_R))):
                in_place = i == 1 and n == 1
                dst_v = view(masked_bias, a - first, b - first)
                src_v = view(masked_bias, a, b) if in_place else view(rel_bias, a, b)
                token = q.issue("gpsimd", lambda e, dst_v=dst_v, src_v=src_v, a=a, b=b, sign=sign, base=base: e.affine_select(
                    out=dst_v, in_=src_v, compare_op=ALU.is_ge, fill=-MASKED, base=base + sign * GRID_R * a,
                    pattern=[[0, 4], [sign * GRID_R, b - a], [0, GRID_R]], channel_multiplier=-sign),
                    after=[bias_here, *bias_read[g], token])
            bias_ready[g] = token

        def add_rel_bias(i, h, scores, dst, after):
            n = scores.shape[1]
            token = q.issue("vector", lambda e: e.scalar_tensor_tensor(dst, scores, SCALE, masked_bias[:, h, 0:n], ALU.mult, ALU.add),
                            after=[*after, bias_ready[h // 4]])
            bias_read[h // 4] = [token]
            if h % 4 == 3 and i + 1 < BLOCKS:
                mask_bias(i + 1, h // 4)
            return token

        attn_b.add_bias = add_rel_bias

        def act_y(hi, lo):
            return lambda k: (hi[:, k, :], lo[:, k, :])

        merged_ready = [()] * KT
        gate_state = {}

        def gate_job(m, n, bias_col, buffer, after):
            result = dense_h()
            slot, temp, free = temps.take()
            z = scaled(result, temp[:, :], after=free)
            token = q.issue("scalar", lambda e: e.activation(buffer[:, n, :], temp[:, :], ACT.Sigmoid, bias=gate_bias[:, bias_col:bias_col + 1]),
                            after=[z, gate_bias_in, *after, *gate_state.get(n, ())])
            release(slot, token)
            gate_state[n] = (token,)

        def merge_a(m, n):
            slot, bank, done = dense(4, n * P, act_y(qa_hi, qa_lo), lambda k: attn_a.out_ready, last_of_unit=n == 1)
            token = q.issue("vector", lambda e: e.tensor_tensor(x[:, m, :], bank[:, :], gates[:, n, :], ALU.mult),
                            after=[done, *gate_state[n], *barrier_x])
            release(slot, token)
            gate_state[n] = (token,)
            merged_ready[m] = (token,)

        barrier_x = [rms_state["sum"]] + [t for m in range(KT) for t in h_ready[m]]
        mask_bias(0, 0)
        mask_bias(0, 1)
        start_beside(attn_b.steps(first=5, period=10,  delay=11))
        for m in range(0, KT, 2):
            for n in range(2):
                gate_job(m + n, n, m + n, gates, after_a)
            for n in range(2):
                merge_a(m + n, n)
        finish_beside()

        after_b = barrier()
        gate_state.clear()

        def merge_b(m, n):
            slot, bank, done = dense(4, n * P, act_y(qb_hi, qb_lo), lambda k: attn_b.out_ready, last_of_unit=n == 1)
            tslot, temp, tfree = temps.take()
            grid = lambda ap: ap.rearrange("p (r c) -> p r c", r=GRID_R)
            part = q.issue("vector", lambda e: e.tensor_tensor(
                grid(temp[:, :]), bank[:, :].rearrange("p (c r) -> p r c", r=GRID_R), grid(gates_b[:, n, :]), ALU.mult),
                after=[done, *gate_state[n], *tfree])
            release(slot, part)
            gate_state[n] = (part,)
            total = q.issue("vector", lambda e: e.tensor_tensor(temp[:, :], temp[:, :], x[:, m, :], ALU.add), after=[part, *merged_ready[m]])
            merged_ready[m] = split_into(temp[:, :], mg_hi[:, m, :], mg_lo[:, m, :], [total])
            release(tslot, *merged_ready[m])
            x_written[m] = (q.dma("gpsimd", lambda e: e.dma_start(x[:, m, :], dram["x"][m * P:(m + 1) * P, :]), x_back[m], after=[total]),)

        lo_engine[0] = "vector"
        for m in range(0, KT, 2):
            for n in range(2):
                gate_job(m + n, n, KT + m + n, gates_b, after_b)
            for n in range(2):
                merge_b(m + n, n)

        def residual(m, result, factor, add_to_norm):
            slot, bank, done = result
            token = q.issue("vector", lambda e: e.scalar_tensor_tensor(x[:, m, :], bank[:, :], factor, x[:, m, :], ALU.mult, ALU.add),
                            after=[done, *x_written[m], *add_to_norm])
            release(slot, token)
            x_written[m] = (token,)

        def out_projection(act, ready, gain, factor=1.0):
            for m in range(KT):
                residual(m, dense(KT, 0, act, ready), factor, ())
                norm_tile(m, gain)

        out_projection(lambda k: (mg_hi[:, k, :], mg_lo[:, k, :]), lambda k: merged_ready[k], 1)

        def mlp(n_tiles, hidden_tile, after, factor, norm):
            ring = Ring([(act_hi[:, n, :], act_lo[:, n, :]) for n in range(ff_ring)])
            ring.users = [tuple(after)] * ff_ring

            def take_hidden():
                slot, (hi, lo), free = ring.take()
                return slot, (hi, lo), hidden_tile(hi, lo, free)

            sizes = [min(FF_CHUNK, n_tiles - s) for s in range(0, n_tiles, FF_CHUNK)]
            held = []

            for c, size in enumerate(sizes):
                if len(held) == c:
                    held.append([])
                while len(held[c]) < size:
                    held[c].append(take_hidden())
                if c + 1 < len(sizes):
                    held.append([take_hidden()])
                tiles = held[c]
                results = []
                if c == len(sizes) - 1:
                    results = dense_pair(size, lambda k: tiles[k][1], lambda k: tiles[k][2])
                for m in range(KT):
                    result = results.pop(0) if results else dense(size, 0, lambda k: tiles[k][1], lambda k: tiles[k][2])
                    residual(m, result, factor, ())
                    if c == len(sizes) - 1:
                        norm(m)
                for slot, _, _ in tiles:
                    release(slot, result[2])

        def relu_squared(hi, lo, free):
            result = dense_h()
            slot, bank, done = result
            s1, positive, f1 = temps.take()
            token = q.issue("vector", lambda e: e.scalar_tensor_tensor(positive[:, :], bank[:, :], 0.0, rms_inv[:, :], ALU.max, ALU.mult),
                            after=[done, rms_state["ready"], *f1])
            release(slot, token)
            s2, squared, f2 = temps.take()
            square = q.issue("scalar", lambda e: e.activation(squared[:, :], positive[:, :], ACT.Square), after=[token, *f2])
            release(s1, square)
            tokens = split_into(squared[:, :], hi, lo, [square], hi_after=free)
            release(s2, *tokens)
            return tokens

        def swiglu(hi, lo, free):
            gate = dense_h()
            s1, temp, f1 = temps.take()
            g = scaled(gate, temp[:, :], after=f1)
            s2, act, f2 = temps.take()
            silu = q.issue("scalar", lambda e: e.activation(act[:, :], temp[:, :], ACT.Silu), after=[g, *f2])
            release(s1, silu)
            up = dense_h()
            s3, value, f3 = temps.take()
            v = scaled(up, value[:, :], after=f3)
            product = q.issue("vector", lambda e: e.tensor_tensor(value[:, :], value[:, :], act[:, :], ALU.mult), after=[v, silu])
            release(s2, product)
            tokens = split_into(value[:, :], hi, lo, [product], hi_after=free)
            release(s3, *tokens)
            return tokens

        pending_norm[0] = norm_finish
        for_both = q.issue("vector", lambda e: e.tensor_tensor(gain_product[:, :], gains[:, 2, :], gains[:, 3, :], ALU.mult),
                           after=[gains_in])

        def norm_tile_twice(m):
            q.wait("scalar", for_both)
            q.wait("vector", for_both)
            h_tile(m, gain_product[:, m:m + 1])
            square_tile(m)
            square_tile(m, scaled_square_sum, "sum_scaled", gains[:, 2, m:m + 1])

        mlp(FF1_TILES, relu_squared, barrier(), 1.0, norm_tile_twice)

        def final_norm(m, gain, scale):
            x_written[m] = (q.issue("vector", lambda e: e.scalar_tensor_tensor(
                x[:, m, :], x[:, m, :], gains[:, gain, m:m + 1], scale[:, :], ALU.mult, ALU.mult),
                after=[*x_written[m], *h_ready[m], *scale_ready]),)

        def norm_and_rescale():
            norm_finish_twice()
            scale_ready[:] = [rms_state["first"], rms_state["sum"], rms_state["sum_scaled"]]
            start_beside([(4 + 4 * m, lambda m=m: final_norm(m, 2, rms_first)) for m in range(KT)])

        scale_ready = []
        pending_norm[0] = norm_and_rescale

        for layer in range(LAYERS_2):
            base = 3 + 3 * layer
            if layer > 0:
                pending_norm[0] = norm_finish
            mlp(FF2_TILES, swiglu, () if layer == 0 else barrier(), 0.5, lambda m: norm_tile(m, base + 1))
            start = barrier()
            padded = q.issue("vector", lambda e: e.memset(conv_u[:, 0:2], 0.0), after=start)
            attn = Attention((q2_hi, q2_lo), (k2_hi, k2_lo), v2, probs_2, probs_t2, out_q2, window_2, chunks_2,
                             add_bias=alibi(dist_2, BLOCK), sink=1 + layer, **gqa)
            pending_norm[0] = norm_finish
            attn.inputs_ready, attn.values_ready = qkv_gqa(q2_hi, q2_lo, k2_hi, k2_lo, v2, after=start)
            attn.probs_ring.users = [tuple(start)] * 3
            attn.turned_ring.users = [tuple(start)] * 2
            conv = {"c": start, "u": [padded], "y": start}
            cat_ready = []

            def conv_c_job():
                conv["c"] = [scaled(dense_h(), conv_c[:, :], after=conv["c"])]

            def conv_h_job(f, layer=layer):
                slot, temp, free = temps.take()
                hz = scaled(dense_h(), temp[:, :], after=free)
                u = q.issue("gpsimd", lambda e: e.tensor_tensor(conv_u[:, 2:TOKENS + 2], temp[:, :], conv_c[:, :], ALU.mult),
                            after=[hz, *conv["c"], *conv["u"]])
                release(slot, u)
                conv["c"] = [u]
                w = lambda k: conv_w[:, layer, f, k:k + 1]

                def own_token():
                    conv["y"] = [q.issue("scalar", lambda e: e.activation(conv_y[:, :], conv_u[:, 2:TOKENS + 2], ACT.Copy, scale=w(2)),
                                         after=[u, padded, conv_w_in, *conv["y"]])]

                def earlier_tokens():
                    for k in (1, 0):
                        conv["y"] = [q.issue("vector", lambda e, k=k: e.scalar_tensor_tensor(
                            conv_y[:, :], conv_u[:, k:k + TOKENS], w(k), conv_y[:, :], ALU.mult, ALU.add), after=[*conv["y"], u, padded])]
                    conv["u"] = list(conv["y"])
                later(3, own_token)
                later(5, earlier_tokens)

            def conv_b_job(f, start=start):
                slot, temp, free = temps.take()
                bz = scaled(dense_h(), temp[:, :], after=free)
                o = q.issue("gpsimd", lambda e: e.tensor_tensor(temp[:, :], temp[:, :], conv_y[:, :], ALU.mult), after=[bz, *conv["y"]])
                conv["y"] = [o]
                cat_ready.append([])
                later(3, lambda: split_later(slot, temp[:, :], cv_hi[:, f, :], cv_lo[:, f, :], cat_ready[f], [o, *start]))

            lo_engine[0] = "gpsimd"
            start_beside(attn.steps(first=5, period=10, delay=11 ))
            for f in range(4):
                conv_c_job()
                conv_h_job(f)
                conv_b_job(f)
            finish_beside()
            lo_engine[0] = "vector"
            cat = [(cv_hi[:, f, :], cv_lo[:, f, :], cat_ready[f]) for f in range(4)]
            cat[3:3] = [(q2_hi[:, t, :], q2_lo[:, t, :], attn.out_ready) for t in range(4)]
            out_projection(lambda k: cat[k][:2], lambda k: cat[k][2], base + 2)
            pending_norm[0] = norm_finish
            last = layer == LAYERS_2 - 1
            mlp(FF2_TILES, swiglu, barrier(), 0.5, lambda m: norm_tile(m, None if last else base + 3))

        norm_finish()
        stores = []
        scale_ready[:] = [rms_state["ready"], rms_state["sum"]]
        for m in range(KT):
            final_norm(m, 9, rms_inv)
            stores.append(q.dma("sync", lambda e, m=m: e.dma_start(out[m * P:(m + 1) * P, :], x[:, m, :]), out_stored, after=x_written[m]))
        q.wait("sync", stores[-1])
        assert current[0] == len(units)

        block = stack.enter_context(nc.Block())
        for name in engines:
            def program(engine, name=name):
                for instruction in q.todo[name]:
                    instruction(engine)
            in_block = {"tensor": block.tensor, "vector": block.vector, "scalar": block.scalar,
                            "gpsimd": block.gpsimd, "sync": block.sync}[name]
            in_block(program)


def plan_units(dram):
    units = []

    def column_tiles(w, tiles):
        units.extend((w[t].rearrange("p k n -> p (k n)"), w.shape[2] * w.shape[3]) for t in tiles)

    def down(w, chunk, size):
        for m in range(KT):
            src = w[m, :, chunk * FF_CHUNK:chunk * FF_CHUNK + size, :].rearrange("p k n -> p (k n)")
            units.append((src, size * P))

    def mlp(ups, w_down, n_tiles):
        n_chunks = -(-n_tiles // FF_CHUNK)
        done = 0
        for c in range(n_chunks):
            size = min(FF_CHUNK, n_tiles - c * FF_CHUNK)
            until = min(n_tiles, c * FF_CHUNK + size + 1)
            for t in range(done, until):
                for w in ups:
                    column_tiles(w, [t])
            done = until
            down(w_down, c, size)

    column_tiles(dram["w_in"], range(18))
    for pair in range(KT // 2):
        column_tiles(dram["w_in"], [18 + 2 * pair, 19 + 2 * pair])
        column_tiles(dram["w_proj_a"], [pair])
    for pair in range(KT // 2):
        column_tiles(dram["w_in"], [26 + 2 * pair, 27 + 2 * pair])
        column_tiles(dram["w_proj_b"], [pair])
    column_tiles(dram["w_out"], range(KT))
    mlp([dram["w_up"]], dram["w_down"], FF1_TILES)
    for layer in range(LAYERS_2):
        mlp([dram["ffn1_wg"][layer], dram["ffn1_wu"][layer]], dram["ffn1_wd"][layer], FF2_TILES)
        column_tiles(dram["w_in_2"][layer], range(18))
        column_tiles(dram["w_out_2"][layer], range(KT))
        mlp([dram["ffn2_wg"][layer], dram["ffn2_wu"][layer]], dram["ffn2_wd"][layer], FF2_TILES)
    return units



def tiled(w, width=P, columns=None, rows=None):
    if rows is not None:
        w = w[rows]
    if columns is not None:
        w = w[:, columns]
    k, n = w.shape
    return np.ascontiguousarray(w.reshape(k // P, P, n // width, width).transpose(2, 1, 0, 3))


def head_order():
    return np.concatenate([np.arange(HEAD) + HEAD * h for m in range(GROUP) for h in (m, m + GROUP)])


def distances():
    query = np.arange(BLOCK)[:, None]
    both = np.abs(query + BLOCK - np.arange(3 * BLOCK)[None, :])
    past = query + BLOCK - np.arange(2 * BLOCK)[None, :]
    return (np.where(both <= BLOCK, both, MASKED).astype(np.float32),
            np.where((past >= 0) & (past < BLOCK), past, MASKED).astype(np.float32))


def kernel(**inputs):
    import concourse.bacc as bacc
    from concourse.bass_utils import run_bass_kernel_spmd

    a = {name: np.asarray(value) for name, value in inputs.items()}
    order = head_order()
    width = HEADS * HEAD
    kv = KV_HEADS * HEAD
    at = np.arange(a["w_in"].shape[2])
    b0 = width + 2 * kv
    cols_1 = [at[width:width + kv], at[width + kv:b0], order]
    for t in range(4):
        cols_1 += [at[b0 + 2 * width + t * P:b0 + 2 * width + (t + 1) * P], at[b0 + width + t * P:b0 + width + (t + 1) * P]]
    cols_1 += [at[b0:b0 + width], at[b0 + 3 * width:]]
    at2 = np.arange(a["w_in_2"].shape[2])
    cols_2 = [at2[width:width + kv], at2[width + kv:b0], order]
    for f in range(4):
        b, c, h = (b0 + n * width + f * P for n in range(3))
        cols_2 += [at2[c:c + P], at2[h:h + P], at2[b:b + P]]
    cols_1, cols_2 = np.concatenate(cols_1), np.concatenate(cols_2)
    rows_2 = np.concatenate([np.arange(width, 2 * width - P), order, np.arange(2 * width - P, 2 * width)])
    both = lambda f, w: np.stack([f(w[layer]) for layer in range(LAYERS_2)])
    column = lambda g: g.reshape(-1, P).T
    gains = [a["norm_mix"][0], a["norm_mlp"][0], a["norm_final"]]
    for layer in range(LAYERS_2):
        gains += [a[n][layer] for n in ("ffn1_norm_2", "mix_norm_2", "ffn2_norm_2")]
    gains.append(a["final_norm_2"])
    dist_1, dist_2 = distances()
    arrays = {
        "x": a["x"][0].T,
        "gains": np.stack([column(g) for g in gains], axis=1),
        "dist_1": dist_1, "dist_2": dist_2, "identity": np.eye(P, dtype=np.float32),
        "gate_bias": column(a["b_gate"][0]),
        "sinks": np.concatenate([a["sink"], a["attn_sink_2"]]),
        "conv_w": a["conv_w_2"].reshape(LAYERS_2, 3, 4, P).transpose(3, 0, 2, 1),
        "rpb": a["rpb"][0],
        "w_in": tiled(a["w_in"][0], columns=cols_1),
        "w_proj_a": tiled(a["w_proj_a"][0], 2 * P, rows=order),
        "w_proj_b": tiled(a["w_proj_b"][0], 2 * P),
        "w_out": tiled(a["w_out"][0]),
        "w_up": tiled(a["w_up"][0]), "w_down": tiled(a["w_down"][0]),
        "w_in_2": both(lambda w: tiled(w, columns=cols_2), a["w_in_2"]),
        "w_out_2": both(lambda w: tiled(w, rows=rows_2), a["w_out_2"]),
    }
    for n in ("ffn1", "ffn2"):
        for w in ("wg", "wu", "wd"):
            arrays[f"{n}_{w}"] = both(tiled, a[f"{n}_{w}_2"])
    arrays = {name: np.ascontiguousarray(v) for name, v in arrays.items()}

    nc = bacc.Bacc("TRN2", target_bir_lowering=False, num_devices=1)
    dram = {name: nc.dram_tensor(f"{name}_dram", v.shape, mybir.dt.from_np(v.dtype), kind="ExternalInput").ap()
            for name, v in arrays.items()}
    dram["rel_scratch"] = nc.dram_tensor("rel_scratch_dram", (GRID_R * HEADS, REL_PAD), F32, kind="Internal").ap()
    out = nc.dram_tensor("out_dram", (D_MODEL, TOKENS), F32, kind="ExternalOutput").ap()
    two_blocks(nc, dram, out)
    result = run_bass_kernel_spmd(nc, [{f"{name}_dram": v for name, v in arrays.items()}], core_ids=[0])
    return np.ascontiguousarray(result.results[0]["out_dram"].T)[None]
```

```python
from contextlib import ExitStack

import numpy as np
from concourse import mybir

F32 = mybir.dt.float32
F32R = mybir.dt.float32r
ALU = mybir.AluOpType
ACT = mybir.ActivationFunctionType
AX_X = mybir.AxisListType.X

P = 128
TOKENS = 512
D_MODEL = 1024
HEAD = 64
HEADS = 8
KV_HEADS = 2
GROUP = HEADS // KV_HEADS
BLOCK = 128
BLOCKS = TOKENS // BLOCK
KT = D_MODEL // P
FF_CHUNK = 8
FF1_TILES = 4096 // P
FF2_TILES = 2816 // P
LAYERS_2 = 2
EPS = 1e-6
EXP_LATER = 2
LO_LATER = 2
SPLIT_LATER = 1
SCALE = HEAD ** -0.5
MASKED = 1e30
UNIT = KT * P
GRID_W = 64
GRID_R = TOKENS // GRID_W
WIN_W = 16
BLOCK_C = BLOCK // GRID_R
SPAN_C = 2 * BLOCK_C
REL_C = 31
REL_PAD = (BLOCK_C - 1 + SPAN_C) * GRID_R


class Semaphore:

    def __init__(self, handle):
        self.handle, self.value = handle, 0

    def next(self, amount):
        self.value += amount
        return (self, self.value)


class Queues:

    def __init__(self, engines):
        self.todo = {name: [] for name in engines}
        self.seen = {name: {} for name in engines}
        self.done = {}

    def wait(self, engine, *tokens):
        highest = {}
        for semaphore, value in (token for token in tokens if token is not None):
            highest[semaphore] = max(value, highest.get(semaphore, 0))
        for semaphore, value in highest.items():
            if value <= self.seen[engine].get(semaphore, 0):
                continue
            self.seen[engine][semaphore] = value
            self.todo[engine].append(lambda e, h=semaphore.handle, v=value: e.wait_ge(h, v))

    def issue(self, engine, make, after=(), signal=True):
        self.wait(engine, *after)
        if not signal:
            self.todo[engine].append(make)
            return None
        token = self.done[engine].next(1)
        self.todo[engine].append(lambda e, h=token[0].handle: make(e).then_inc(h, 1))
        return token

    def dma(self, engine, make, semaphore, after=()):
        self.wait(engine, *after)
        token = semaphore.next(16)
        self.todo[engine].append(lambda e, h=semaphore.handle: make(e).then_inc(h, 16))
        return token


class Ring:

    def __init__(self, buffers):
        self.buffers, self.users, self.at = list(buffers), [()] * len(buffers), -1

    def take(self):
        self.at = (self.at + 1) % len(self.buffers)
        free, self.users[self.at] = self.users[self.at], None
        assert free is not None, "still in use"
        return (self, self.at), self.buffers[self.at], free


def release(slot, *tokens):
    ring, at = slot
    ring.users[at] = tokens


def two_blocks(nc, dram, out):
    engines = ("tensor", "vector", "scalar", "gpsimd", "sync")
    q = Queues(engines)
    stack = ExitStack()
    with stack:
        def sbuf(name, shape, dt=F32, on=stack):
            return on.enter_context(nc.sbuf_tensor(name, shape, dt))

        def semaphore(name):
            return Semaphore(stack.enter_context(nc.semaphore(name)))

        x = sbuf("x", [P, KT, TOKENS])
        h_hi = sbuf("h_hi", [P, KT, TOKENS], F32R)
        h_lo = sbuf("h_lo", [P, KT, TOKENS], F32R)
        n_units = 3
        w_raw = [sbuf(f"w_raw{i}", [P, UNIT]) for i in range(n_units)]
        w_hi = [sbuf(f"w_hi{i}", [P, UNIT], F32R) for i in range(n_units)]
        w_lo = [sbuf(f"w_lo{i}", [P, UNIT], F32R) for i in range(n_units)]
        rms_inv = sbuf("rms_inv", [P, TOKENS])
        square_sum = sbuf("square_sum", [P, TOKENS])
        temps = Ring([sbuf(f"temp{i}", [P, TOKENS]) for i in range(5)])
        identity = sbuf("identity", [P, P])
        ones = sbuf("ones", [P, P])
        dist_1 = sbuf("dist_1", [P, 3 * BLOCK])
        eps_col = sbuf("eps_col", [P, 1])
        root_ready = sbuf("root_ready", [P, 1])
        gains = sbuf("gains", [P, 10, KT])
        gain_product = sbuf("gain_product", [P, KT])
        gate_bias = sbuf("gate_bias", [P, 2 * KT])
        sinks = sbuf("sinks", [P, 3, HEADS])
        sinks_8 = sbuf("sinks_8", [P, 3, HEADS])
        conv_w = sbuf("conv_w", [P, LAYERS_2, 4, 3])
        row_max = sbuf("row_max", [P, 2, HEADS])
        neg_max = sbuf("neg_max", [P, 2, HEADS])
        sink_shift = sbuf("sink_shift", [P, 2, HEADS])
        sink_exp = sbuf("sink_exp", [P, 2, HEADS])
        row_sum = sbuf("row_sum", [P, 2, HEADS])
        row_inv = sbuf("row_inv", [P, 2, HEADS])

        def phase(tensors, on):
            return [sbuf(n, s, d, on) for n, s, d in tensors]

        ff_phase, mix1, mix2 = ExitStack(), ExitStack(), ExitStack()
        ff_ring = FF_CHUNK + 2
        with ff_phase:
            act_hi, act_lo = phase([("act_hi", [P, ff_ring, TOKENS], F32R), ("act_lo", [P, ff_ring, TOKENS], F32R)], ff_phase)
            scaled_square_sum, rms_first = phase([("scaled_square_sum", [P, TOKENS], F32), ("rms_first", [P, TOKENS], F32)], ff_phase)
        with mix1:
            (qa,) = phase([("qa", [P, HEADS, TOKENS], F32R)], mix1)
            qb_hi, qb_lo = phase([("qb_hi", [P, 4, TOKENS], F32R), ("qb_lo", [P, 4, TOKENS], F32R)], mix1)
            probs_t1, out_q1, probs_1 = phase([
                ("probs_t1", [P, 2, TOKENS], F32), ("out_q1", [P, TOKENS], F32),
                ("probs_1", [P, 3, GROUP, 3 * BLOCK], F32)], mix1)
            with ExitStack() as kv_part:
                kb_hi, kb_lo = phase([("kb_hi", [P, 4, TOKENS], F32R), ("kb_lo", [P, 4, TOKENS], F32R)], kv_part)
                (vb,) = phase([("vb", [P, BLOCKS + 1, HEADS, HEAD], F32)], kv_part)
                rel_bias, masked_bias = phase([("rel_bias", [P, HEADS, 2 * BLOCK], F32),
                                               ("masked_bias", [P, HEADS, 2 * BLOCK], F32)], kv_part)
                with ExitStack() as part_a:
                    ka_hi, ka_lo, va = phase([("ka_hi", [P, KV_HEADS, TOKENS], F32R), ("ka_lo", [P, TOKENS], F32R),
                                              ("va", [P, BLOCKS, KV_HEADS, HEAD], F32)], part_a)
                with ExitStack() as part_b:
                    (gates,) = phase([("gates", [P, 2, TOKENS], F32)], part_b)
            with ExitStack() as part_m:
                mg_hi, mg_lo, gates_b = phase([("mg_hi", [P, KT, TOKENS], F32R), ("mg_lo", [P, KT, TOKENS], F32R),
                                               ("gates_b", [P, 2, TOKENS], F32)], part_m)
        with mix2:
            q2, dist_2 = phase([("q2", [P, HEADS, TOKENS], F32R), ("dist_2", [P, 2 * BLOCK], F32)], mix2)
            k2_hi, k2_lo, v2 = phase([("k2_hi", [P, KV_HEADS, TOKENS], F32R), ("k2_lo", [P, TOKENS], F32R),
                                      ("v2", [P, BLOCKS, KV_HEADS, HEAD], F32)], mix2)
            probs_t2, out_q2, probs_2 = phase([
                ("probs_t2", [P, 2, TOKENS], F32), ("out_q2", [P, TOKENS], F32),
                ("probs_2", [P, 3, GROUP, 2 * BLOCK], F32)], mix2)
            cv_hi, cv_lo = phase([("cv_hi", [P, 4, TOKENS], F32R), ("cv_lo", [P, 4, TOKENS], F32R)], mix2)
            conv_c, conv_u, conv_y = phase([("conv_c", [P, TOKENS], F32), ("conv_u", [P, TOKENS + 2], F32),
                                            ("conv_y", [P, TOKENS], F32)], mix2)

        psum = [stack.enter_context(nc.psum_tensor(f"bank{i}", [P, TOKENS], F32)) for i in range(8)]
        dense_banks, score_banks, turn_banks = Ring(psum[0:3]), Ring(psum[3:5]), Ring(psum[5:7])
        value_bank = Ring(psum[7:8])

        for name in engines[:4]:
            q.done[name] = semaphore(f"{name}_done")
        landed = [semaphore(f"weights_landed{i}") for i in range(n_units)]
        consts_landed = [semaphore(f"consts_landed{i}") for i in range(8)]
        x_landed = [semaphore(f"x_landed{i}") for i in range(KT)]
        x_back = [semaphore(f"x_back{i}") for i in range(KT)]
        rel_landed = semaphore("rel_landed")
        rel_stored = semaphore("rel_stored")
        bias_landed = semaphore("bias_landed")
        out_stored = semaphore("out_stored")

        def barrier():
            return [(s, s.value) for s in q.done.values() if s.value]

        def load_const(i, dst, src, after=()):
            return q.dma("sync", lambda e: e.dma_start(dst, src), consts_landed[i], after=after)

        ones_ready = q.issue("vector", lambda e: e.memset(ones[:, :], 1.0))
        eps_ready = q.issue("vector", lambda e: e.memset(eps_col[:, :], EPS))

        unit_ready = []
        raw_free = [()] * n_units
        split_free = [()] * n_units
        units = plan_units(dram)
        lo_engine = ["vector"]
        fetched = {}

        def fetch_unit(u):
            if u in fetched:
                return fetched[u]
            s, (src, width) = u % n_units, units[u]
            fetched[u] = q.dma("sync", lambda e: e.dma_start(w_raw[s][:, 0:width], src), landed[s], after=raw_free[s])
            return fetched[u]

        gains_in = load_const(0, gains[:, :, :], dram["gains"])
        x_ready = []
        for m in range(KT):
            x_ready.append(q.dma("sync", lambda e, m=m: e.dma_start(x[:, m, :], dram["x"][m * P:(m + 1) * P, :]), x_landed[m]))
            if m < n_units:
                fetch_unit(m)
        identity_in = load_const(3, identity[:, :], dram["identity"])
        dist1_in = load_const(1, dist_1[:, :], dram["dist_1"])
        sinks_in = load_const(5, sinks[:, :, :], dram["sinks"].partition_broadcast(P))
        gate_bias_in = load_const(4, gate_bias[:, :], dram["gate_bias"])
        conv_w_in = load_const(6, conv_w[:, :, :, :], dram["conv_w"])

        def split_unit(u):
            s, width = u % n_units, units[u][1]
            raw_here = fetch_unit(u)
            hi = q.issue("scalar", lambda e: e.activation(w_hi[s][:, 0:width], w_raw[s][:, 0:width], ACT.Copy),
                         after=[raw_here, *split_free[s]])
            lo = q.issue(lo_engine[0], lambda e: e.tensor_tensor(w_lo[s][:, 0:width], w_raw[s][:, 0:width],
                                                                 w_hi[s][:, 0:width].bitcast(F32), ALU.subtract),
                         after=[hi, raw_here, *split_free[s]])
            raw_free[s] = (lo,)
            unit_ready.append(lo)

        current = [0]
        first_results = []
        beside = {"slot": 0, "steps": []}

        def start_beside(steps):
            beside["steps"] = sorted(beside["steps"] + [(beside["slot"] + at, step) for at, step in steps], key=lambda s: s[0])

        def later(slots, step):
            start_beside([(slots, step)])

        def next_slot():
            while beside["steps"] and beside["steps"][0][0] <= beside["slot"]:
                beside["steps"].pop(0)[1]()
            beside["slot"] += 1

        def finish_beside():
            while beside["steps"]:
                beside["steps"].pop(0)[1]()

        def dense(k_tiles, columns, act, ready, last_of_unit=True, banks=dense_banks):
            u = current[0]
            slot, bank, bank_free = banks.take()
            q.wait("tensor", unit_ready[u], *bank_free)
            for k in range(k_tiles):
                q.wait("tensor", *ready(k))
                token = k_step(u, bank, k, k_tiles, columns, act)
                if k < k_tiles - 1:
                    next_slot()
            if last_of_unit:
                next_unit(token)
            next_slot()
            return slot, bank, token

        def dense_pair(k_tiles, act, ready):
            u, taken, results = current[0], [dense_banks.take() for _ in range(2)], []
            for ks in (range(k_tiles - 1), (k_tiles - 1,)):
                for n, (_, bank, bank_free) in enumerate(taken):
                    q.wait("tensor", unit_ready[u + n], *bank_free)
                    for k in ks:
                        q.wait("tensor", *ready(k))
                        token = k_step(u + n, bank, k, k_tiles, 0, act)
                        if k == k_tiles - 1:
                            results.append((taken[n][0], bank, token))
                            next_unit(token, 0)
                        next_slot()
            return results

        def k_step(u, bank, k, k_tiles, columns, act):
            s, width = u % n_units, units[u][1] // k_tiles
            hi, lo = act(k)
            lhs = slice(k * width + columns, k * width + columns + P)
            for n, (w, a) in enumerate(((w_hi[s], hi), (w_hi[s], lo), (w_lo[s], hi))):
                first, last = k == 0 and n == 0, k == k_tiles - 1 and n == 2
                token = q.issue("tensor", lambda e, w=w, a=a, first=first, last=last: e.matmul(
                    bank[:, :], w[:, lhs], a, start=first, stop=last), signal=last)
            return token

        def next_unit(token, slots=SPLIT_LATER):
            u = current[0]
            split_free[u % n_units] = (token,)
            current[0] += 1
            if u + n_units < len(units):
                fetch_unit(u + n_units)
                later(slots, lambda: split_unit(u + n_units))

        def dense_first():
            results = [dense_banks.take() for _ in range(n_units)]
            for k in range(KT):
                h_tile(k, gains[:, 0, k:k + 1])
                if k < n_units:
                    split_unit(k)
                if k >= 2:
                    square_tile(k - 2)
            for k in (KT - 2, KT - 1):
                square_tile(k)

            def steps(u, ks):
                q.wait("tensor", unit_ready[u])
                for k in ks:
                    q.wait("tensor", *h_ready[k])
                    token = k_step(u, results[u][1], k, KT, 0, act_h)
                return token

            side_by_side = KT // 2
            for k in range(side_by_side):
                for u in range(n_units):
                    steps(u, [k])
            for u in range(n_units):
                if u == n_units - 1:
                    norm_finish()
                token = steps(u, range(side_by_side, KT))
                first_results.append((*results[u][:2], token))
                next_unit(token)
                for _ in range(SPLIT_LATER + 1):
                    next_slot()
            first_results.append(dense(KT, 0, act_h, lambda k: h_ready[k], banks=score_banks))
            h_read[0] = (first_results[-1][2],)

        def act_h(k):
            return h_hi[:, k, :], h_lo[:, k, :]

        h_ready = [()] * KT
        h_read = [()]
        x_written = [(t,) for t in x_ready]
        rms_state = {"ready": None, "sum": None, "sum_scaled": None}

        pending_norm = [None]

        def dense_h():
            if first_results:
                return first_results.pop(0)
            result = dense(KT, 0, act_h, lambda k: h_ready[k])
            h_read[0] = (result[2],)
            if pending_norm[0]:
                pending_norm[0]()
                pending_norm[0] = None
            return result

        def split_into(value, hi, lo, after, hi_after=()):
            hi_done = q.issue("scalar", lambda e: e.activation(hi, value, ACT.Copy), after=[*after, *hi_after])
            lo_done = q.issue("vector", lambda e: e.tensor_tensor(lo, value, hi.bitcast(F32), ALU.subtract),
                              after=[hi_done, *after, *hi_after])
            return (lo_done,)

        def h_tile(m, g):
            after = [*x_written[m], gains_in]
            hi = q.issue("scalar", lambda e: e.activation(h_hi[:, m, :], x[:, m, :], ACT.Copy, scale=g), after=[*after, *h_read[0]])
            lo = q.issue("vector", lambda e: e.scalar_tensor_tensor(h_lo[:, m, :], x[:, m, :], g, h_hi[:, m, :].bitcast(F32),
                                                                    ALU.mult, ALU.subtract), after=[hi, *after, *h_read[0]])
            h_ready[m] = (lo,)

        def square_tile(m, into=square_sum, state="sum", scale=1.0):
            if m == 0:
                rms_state[state] = q.issue("scalar", lambda e: e.activation(into[:, :], x[:, m, :], ACT.Square, scale=scale),
                                           after=[*x_written[m], rms_state[state]])
                return
            slot, temp, free = temps.take()
            squared = q.issue("scalar", lambda e: e.activation(temp[:, :], x[:, m, :], ACT.Square, scale=scale),
                              after=[*x_written[m], *free])
            rms_state[state] = q.issue("gpsimd", lambda e: e.tensor_tensor(into[:, :], into[:, :], temp[:, :], ALU.add),
                                       after=[squared, rms_state[state]])
            release(slot, rms_state[state])

        def norm_tile(m, gain):
            if gain is not None:
                h_tile(m, gains[:, gain, m:m + 1])
            square_tile(m)

        def sum_partitions(ring, state="sum", source=square_sum):
            slot, bank, free = ring.take()
            summed = q.issue("tensor", lambda e: e.matmul(bank[:, :], ones[:, :], source[:, :], start=True, stop=True),
                             after=[rms_state[state], ones_ready, *free])
            rms_state[state] = summed
            return slot, bank, summed

        def inverse_root(dst, value, scale, bias, after, before=()):
            tslot, temp, tfree = temps.take()
            root = q.issue("scalar", lambda e: e.activation(temp[:, :], value, ACT.Sqrt, bias=bias, scale=scale),
                           after=[*after, eps_ready, *tfree])
            done = q.issue("vector", lambda e: e.reciprocal(dst[:, :], temp[:, :]), after=[root, *before])
            release(tslot, done)
            return root, done

        def norm_finish():
            slot, bank, summed = sum_partitions(value_bank)
            root, rms_state["ready"] = inverse_root(rms_inv, bank[:, :], 1 / D_MODEL, eps_col[:, :], [summed], [rms_state["ready"]])
            release(slot, root)

        def norm_finish_twice():
            slot1, bank1, summed1 = sum_partitions(value_bank)
            slot2, bank2, summed2 = sum_partitions(turn_banks, "sum_scaled", scaled_square_sum)
            tslot, temp, tfree = temps.take()
            part = q.issue("vector", lambda e: e.tensor_scalar(temp[:, :], bank1[:, :], EPS / D_MODEL, EPS * EPS, ALU.mult, ALU.add),
                           after=[summed1, *tfree])
            value = q.issue("vector", lambda e: e.scalar_tensor_tensor(temp[:, :], bank2[:, :], 1 / D_MODEL, temp[:, :], ALU.mult, ALU.add),
                            after=[summed2, part])
            root, rms_state["ready"] = inverse_root(rms_inv, temp[:, :], 1.0, 0.0, [value], [rms_state["ready"]])
            release(slot2, value)
            release(tslot, root)

            def first_scale():
                first_root, rms_state["first"] = inverse_root(rms_first, bank1[:, :], 1 / D_MODEL, eps_col[:, :], [summed1, part])
                release(slot1, first_root)
            return first_scale

        def scaled(result, dst, view=None, after=()):
            slot, bank, done = result
            src, scale = bank[:, :], rms_inv[:, :]
            if view is not None:
                src, scale, dst = view(src), view(scale), dst.rearrange("p (c r) -> p c r", r=GRID_R)
            token = q.issue("vector", lambda e: e.tensor_tensor(dst, src, scale, ALU.mult),
                            after=[done, rms_state["ready"], *after])
            release(slot, token)
            return token

        def by_column(ap):
            return ap.rearrange("p (r c) -> p c r", r=GRID_R)

        def split_later(slot, value, hi, lo, ready, after):
            hi_done = q.issue("scalar", lambda e: e.activation(hi, value, ACT.Copy), after=after)

            def rest():
                lo_done = q.issue("vector", lambda e: e.tensor_tensor(lo, value, hi.bitcast(F32), ALU.subtract), after=[hi_done, *after])
                ready.append(lo_done)
                release(slot, lo_done)
            later(LO_LATER, rest)

        def project_split(hi, lo, ready, view=None, after=()):
            result = dense_h()
            slot, temp, free = temps.take()
            z = scaled(result, temp[:, :], view, after=free)
            split_later(slot, temp[:, :], hi, lo, ready, [z, *after])

        def project_v(dst, heads, chunks, view=None, after=()):
            result = dense_h()
            slot, temp, free = temps.take()
            z = scaled(result, temp[:, :], view, after=free)
            ready = []

            def turn(c0):
                part = chunks[c0:c0 + 4]
                bslot, bank, bfree = turn_banks.take()
                q.wait("tensor", z, identity_in, *bfree)
                for n, (start, rows) in enumerate(part):
                    turned = q.issue("tensor", lambda e, n=n, start=start, rows=rows: e.transpose(
                        bank[0:rows, n * P:(n + 1) * P], temp[:, start:start + rows], identity[:, :]),
                        signal=n == len(part) - 1)
                runs = []
                for n, (_, rows) in enumerate(part):
                    if runs and runs[-1][2] == rows:
                        runs[-1][1] = n + 1
                    else:
                        runs.append([n, n + 1, rows])
                for a, b, rows in runs:
                    src = bank[0:rows, a * P:b * P].rearrange("p (c h d) -> p c h d", c=b - a, h=2)
                    d = dst[0:rows, c0 + a:c0 + b, heads[0]:heads[0] + 2, :]
                    copied = q.issue("scalar", lambda e, src=src, d=d: e.activation(d, src, ACT.Copy), after=[turned, *after])
                release(bslot, copied)
                ready.append(copied)
                if c0 + 4 >= len(chunks):
                    release(slot, turned)
            return ready, [lambda c0=c0: turn(c0) for c0 in range(0, len(chunks), 4)]

        class Attention:

            def __init__(self, products, y_hi, y_lo, values, probs, turned, out_q, key_range, chunks, place, value_head,
                         add_bias, exp_scale, sink):
                self.products, self.y_hi, self.y_lo, self.place = products, y_hi, y_lo, place
                self.values, self.out_q = values, out_q
                self.key_range, self.chunks = key_range, chunks
                self.value_head = value_head
                self.add_bias, self.exp_scale, self.sink = add_bias, exp_scale, sink
                self.probs_ring = Ring([probs[:, n] for n in range(3)])
                self.turned_ring = Ring([turned[:, n] for n in range(2)])
                self.inputs_ready, self.values_ready, self.out_ready = [], [], []
                self.group = {}
                self.block = {}
                self.out_q_read = None

            def by_place(self, stats, i, g):
                first, step = self.place(4 * g), self.place(4 * g + 1) - self.place(4 * g)
                return stats[:, i % 2, first:first + 3 * step + 1:step]

            def score(self, i, g, n):
                h, (start, count) = 4 * g + n, self.key_range[i]
                if n == 0:
                    slot, probs, free = self.probs_ring.take()
                    self.group[i, g] = {"slot": slot, "probs": probs, "free": free}
                state = self.group[i, g]
                cols = slice(i * BLOCK, (i + 1) * BLOCK)
                slot, bank, free = score_banks.take()
                q.wait("tensor", *free, *self.inputs_ready)
                pairs = self.products(h)
                for m, (queries, keys) in enumerate(pairs):
                    last = m == len(pairs) - 1
                    done = q.issue("tensor", lambda e, queries=queries, keys=keys, m=m, last=last: e.matmul(
                        bank[:, 0:count], queries[:, cols], keys[:, start:start + count], start=m == 0, stop=last), signal=last)
                scored = self.add_bias(i, h, bank[:, 0:count], state["probs"][:, n, 0:count], [done, *state["free"]])
                release(slot, scored)
                if n == GROUP - 1:
                    self.softmax(i, g, scored)

            def softmax(self, i, g, scored):
                state, count = self.group[i, g], self.key_range[i][1]
                probs, heads = state["probs"], slice(4 * g, 4 * g + 4)
                top, neg, shift = (a[:, i % 2, heads] for a in (row_max, neg_max, sink_shift))
                done = q.issue("vector", lambda e: e.tensor_reduce(top, probs[:, :, 0:count], AX_X, ALU.max),
                               after=[scored, self.block.get(i - 2)])
                if self.sink is not None:
                    done = q.issue("vector", lambda e: e.tensor_tensor(top, top, sinks_8[:, self.sink, heads], ALU.max),
                                   after=[done, sinks8_ready])
                done = q.issue("vector", lambda e: e.tensor_scalar(neg, top, -self.exp_scale, None, ALU.mult), after=[done])
                if self.sink is not None:
                    shifted = q.issue("vector", lambda e: e.tensor_tensor(shift, sinks[:, self.sink, heads], neg, ALU.add),
                                      after=[done])

                def exponentials():
                    for n in range(GROUP):
                        p, s = probs[:, n, 0:count], self.place(4 * g + n)
                        exps = q.issue("scalar", lambda e, p=p, n=n, s=s: e.activation(
                            p, p, ACT.Exp, bias=neg[:, n:n + 1], scale=self.exp_scale, accum_out=row_sum[:, i % 2, s:s + 1]),
                            after=[done, self.block.get(i - 2)])
                    if self.sink is not None:
                        exps = q.issue("scalar", lambda e: e.activation(self.by_place(sink_exp, i, g), shift, ACT.Exp),
                                       after=[shifted])
                    state["exps"] = exps
                later(EXP_LATER, exponentials)

            def turn(self, i, g, c):
                state = self.group[i, g]
                _, offset, rows = self.chunks[i][c]
                bslot, bank, bfree = turn_banks.take()
                q.wait("tensor", state["exps"], identity_in, *bfree)
                for n in range(GROUP):
                    turned = q.issue("tensor", lambda e, n=n: e.transpose(
                        bank[0:rows, n * P:(n + 1) * P], state["probs"][:, n, offset:offset + rows], identity[:, :]),
                        signal=n == 3)
                slot, dst, free = self.turned_ring.take()
                copied = q.issue("scalar", lambda e: e.activation(dst[0:rows, :], bank[0:rows, :], ACT.Copy), after=[turned, *free])
                release(bslot, copied)
                state[c] = (slot, dst, copied)
                if c == len(self.chunks[i]) - 1:
                    release(state["slot"], turned)

            def multiply(self, i, g, c):
                slot, turned, copied = self.group[i, g][c]
                value_chunk, _, rows = self.chunks[i][c]
                if g == 0 and c == 0:
                    self.value_slot, self.value_bank, free = value_bank.take()
                    q.wait("tensor", *free)
                bank = self.value_bank
                q.wait("tensor", copied, *self.values_ready)
                last_chunk = c == len(self.chunks[i]) - 1
                for n in range(GROUP):
                    h = 4 * g + n
                    cols = slice(HEAD * self.place(h), HEAD * self.place(h) + HEAD)
                    done = q.issue("tensor", lambda e, n=n, h=h, cols=cols: e.matmul(
                        bank[:, cols], turned[0:rows, n * P:(n + 1) * P], self.values[0:rows, value_chunk, self.value_head(h), :],
                        start=g == 0 and c == 0 and n == 0, stop=last_chunk, skip_group_check=True), signal=n == 3)
                release(slot, done)
                if g == 1 and last_chunk:
                    self.normalise(i, done)

            def normalise(self, i, done):
                total, inv, bank = row_sum[:, i % 2, :], row_inv[:, i % 2, :], self.value_bank
                ready = [self.group[i, 0]["exps"], self.group[i, 1]["exps"]]
                if self.sink is not None:
                    ready = [q.issue("vector", lambda e: e.tensor_tensor(total, total, sink_exp[:, i % 2, :], ALU.add), after=ready)]
                inverse = q.issue("vector", lambda e: e.reciprocal(inv, total), after=ready)
                heads = lambda ap: ap.rearrange("p (h d) -> p h d", d=HEAD)
                self.block[i] = q.issue("vector", lambda e: e.tensor_tensor(
                    heads(self.out_q[:, :]), heads(bank[:, :]), inv.unsqueeze(2).broadcast_to([P, HEADS, HEAD]), ALU.mult),
                    after=[inverse, done, self.out_q_read])
                release(self.value_slot, self.block[i])

            def turn_out(self, i):
                bslot, bank, bfree = turn_banks.take()
                q.wait("tensor", self.block[i], identity_in, *bfree)
                for t in range(4):
                    turned = q.issue("tensor", lambda e, t=t: e.transpose(
                        bank[:, t * P:(t + 1) * P], self.out_q[:, t * P:(t + 1) * P], identity[:, :]), signal=t == 3)
                self.out_q_read = turned
                cols = slice(i * BLOCK, (i + 1) * BLOCK)
                src = bank[:, :].rearrange("p (t n) -> p t n", t=4)
                hi, lo = self.y_hi[:, :, cols], self.y_lo[:, :, cols]
                hi_done = q.issue("scalar", lambda e: e.activation(hi, src, ACT.Copy), after=[turned])

                def rest():
                    lo_done = q.issue("vector", lambda e: e.tensor_tensor(lo, src, hi.bitcast(F32), ALU.subtract), after=[hi_done])
                    release(bslot, lo_done)
                    self.out_ready.append(lo_done)
                later(1, rest)

            def steps(self, first, period, delay):
                steps = []
                for i in range(BLOCKS):
                    for g in range(2):
                        at = first + period * (2 * i + g)
                        steps += [(at + n, lambda i=i, g=g, n=n: self.score(i, g, n)) for n in range(GROUP)]
                        chunks = range(len(self.chunks[i]))
                        steps += [(at + delay + 2 * c, lambda i=i, g=g, c=c: self.turn(i, g, c)) for c in chunks]
                        steps += [(at + delay + 3 + 2 * c, lambda i=i, g=g, c=c: self.multiply(i, g, c)) for c in chunks]
                    steps.append((at + delay + 2 * len(chunks) + 5, lambda i=i: self.turn_out(i)))
                return steps

        def alibi(dist, dist_in, first_offset):
            def add_bias(i, h, scores, dst, after):
                n = scores.shape[1]
                lo = first_offset if i == 0 else 0
                slope = 2.0 ** -(h + 1)
                return q.issue("vector", lambda e: e.scalar_tensor_tensor(dst, dist[:, lo:lo + n], -slope / SCALE, scores, ALU.mult, ALU.add),
                               after=[*after, dist_in])
            return add_bias

        window_1 = [(max(0, i - 1) * BLOCK, (min(BLOCKS, i + 2) - max(0, i - 1)) * BLOCK) for i in range(BLOCKS)]
        chunks_1 = [[(s // BLOCK + c, c * BLOCK, BLOCK) for c in range(n // BLOCK)] for s, n in window_1]
        window_2 = [(max(0, i - 1) * BLOCK, (i + 1 - max(0, i - 1)) * BLOCK) for i in range(BLOCKS)]
        chunks_2 = [[(s // BLOCK + c, c * BLOCK, BLOCK) for c in range(n // BLOCK)] for s, n in window_2]

        def half(n):
            return slice(HEAD * n, HEAD * n + HEAD)

        def gqa_parts(queries, k_hi, k_lo):
            return dict(products=lambda h: ((queries[:, h, :], k_hi[:, h // GROUP, :]),
                                            (queries[half(h // GROUP), h, :], k_lo[half(h // GROUP), :])),
                        y_hi=queries[:, 0:4, :], y_lo=queries[:, 4:8, :],
                        place=lambda h: 2 * (h % GROUP) + h // GROUP, value_head=lambda h: h // GROUP, exp_scale=SCALE)

        def project_stacked(copy_hi, lo_of, ready, after):
            result = dense_h()
            slot, temp, free = temps.take()
            z = scaled(result, temp[:, :], after=free)
            for n, hi in copy_hi:
                hi_done = q.issue("scalar", lambda e, n=n, hi=hi: e.activation(hi, temp[half(n), :], ACT.Copy), after=[z, *after])

            def rest():
                for n, hi, lo in lo_of:
                    lo_done = q.issue("vector", lambda e, n=n, hi=hi, lo=lo: e.tensor_tensor(
                        lo, temp[half(n), :], hi.bitcast(F32), ALU.subtract), after=[hi_done, *after])
                ready.append(lo_done)
                release(slot, lo_done)
            later(LO_LATER, rest)

        half_block = BLOCK // 2
        window_b = [(0, BLOCK + half_block)] + [(i * BLOCK - half_block, 2 * BLOCK) for i in (1, 2)] + \
                   [((BLOCKS - 1) * BLOCK - half_block, BLOCK + half_block)]
        value_chunks_b = [(0, half_block)] + [(j * BLOCK - half_block, BLOCK) for j in range(1, BLOCKS)] + \
                         [(TOKENS - half_block, half_block)]
        chunks_b = []
        for i in range(BLOCKS):
            a, b = value_chunks_b[i], value_chunks_b[i + 1]
            chunks_b.append([(i, 0, a[1]), (i + 1, a[1], b[1])])

        dense_first()
        sinks8_ready = q.issue("vector", lambda e: e.tensor_scalar(sinks_8[:, :, :], sinks[:, :, :], 1 / SCALE, None, ALU.mult),
                               after=[sinks_in])

        rel_rows = 8 * HEADS
        rel_in_slot, rel_in, rel_in_free = temps.take()
        for r in range(GRID_R):
            rel_here = q.dma("gpsimd", lambda e, r=r: e.dma_start(
                rel_in[r * HEADS:(r + 1) * HEADS, 0:GRID_R * REL_C].rearrange("h (a b) -> h a b", a=GRID_R),
                dram["rpb"][:, GRID_R - 1 - r:2 * GRID_R - 1 - r, :]), rel_landed, after=rel_in_free if r == 0 else ())
        rel_out_slot, rel_out, rel_out_free = temps.take()
        cleared = q.issue("gpsimd", lambda e: e.memset(rel_out[0:rel_rows, 0:REL_PAD], 0.0), after=rel_out_free)
        pad = 8 * GRID_R
        spread = q.issue("gpsimd", lambda e: e.tensor_copy(
            rel_out[0:rel_rows, pad:pad + REL_C * GRID_R].rearrange("p (d r) -> p d r", r=GRID_R),
            rel_in[0:rel_rows, 0:GRID_R * REL_C].rearrange("p (r d) -> p d r", r=GRID_R)), after=[rel_here, cleared])
        rel_kept = q.dma("sync", lambda e: e.dma_start(dram["rel_scratch"], rel_out[0:rel_rows, 0:REL_PAD]), rel_stored, after=[spread])
        release(rel_in_slot, spread)
        release(rel_out_slot, rel_kept)
        for c in range(BLOCK_C):
            off = (BLOCK_C - 1 - c) * GRID_R
            bias_here = q.dma("gpsimd", lambda e, c=c, off=off: e.dma_start(
                rel_bias[c * GRID_R:(c + 1) * GRID_R, :, :],
                dram["rel_scratch"].rearrange("(r h) x -> r h x", h=HEADS)[:, :, off:off + 2 * BLOCK]),
                bias_landed, after=[rel_kept])

        chunks_v = [(j * BLOCK, BLOCK) for j in range(BLOCKS)]

        def qkv_gqa(queries, k_hi, k_lo, v, after=(), after_v=9):
            ready = []
            project_stacked([(kv, k_hi[half(to), kv, :]) for kv in range(KV_HEADS) for to in range(2)],
                            [(kv, k_hi[half(kv), kv, :], k_lo[half(kv), :]) for kv in range(KV_HEADS)], ready, after)
            v_ready, turns = project_v(v, (0, 1), chunks_v, after=after)
            start_beside([(after_v + n, turn) for n, turn in enumerate(turns)])
            for t in range(4):
                tile = [queries[:, t, :], queries[:, GROUP + t, :]]
                project_stacked([(n, tile[n][half(n), :]) for n in range(2)],
                                [(n, tile[n][half(n), :], tile[n][half(1 - n), :]) for n in range(2)], ready, after)
            return ready, v_ready

        attn_a = Attention(values=va, probs=probs_1, turned=probs_t1, out_q=out_q1, key_range=window_1, chunks=chunks_1,
                           add_bias=alibi(dist_1, dist1_in, BLOCK), sink=0, **gqa_parts(qa, ka_hi, ka_lo))
        attn_a.inputs_ready, attn_a.values_ready = qkv_gqa(qa, ka_hi, ka_lo, va, after_v=1)

        attn_b = Attention(products=lambda h: [(qs[half(h % 2), h // 2, :], ks[half(h % 2), h // 2, :])
                                               for qs, ks in ((qb_hi, kb_hi), (qb_hi, kb_lo), (qb_lo, kb_hi))],
                           y_hi=qb_hi, y_lo=qb_lo, values=vb, probs=probs_1, turned=probs_t1, out_q=out_q1,
                           key_range=window_b, chunks=chunks_b, place=lambda h: h, value_head=lambda h: h,
                           add_bias=None, exp_scale=1.0, sink=None)
        vb_tokens = []
        lo_engine[0] = "gpsimd"
        start_beside(attn_a.steps(first=7, period=10, delay=11))
        for t in range(4):
            ready, turns = project_v(vb, (2 * t, 2 * t + 1), value_chunks_b, view=by_column)
            vb_tokens.append(ready)
            start_beside([(6 + 2 * n, turn) for n, turn in enumerate(turns)])
            project_split(kb_hi[:, t, :], kb_lo[:, t, :], attn_b.inputs_ready, view=by_column)
        for t in range(4):
            project_split(qb_hi[:, t, :], qb_lo[:, t, :], attn_b.inputs_ready, view=by_column)
        finish_beside()

        after_a = barrier()
        attn_b.values_ready = [t for ready in vb_tokens for t in ready]
        attn_b.probs_ring.users = attn_a.probs_ring.users
        attn_b.turned_ring.users = attn_a.turned_ring.users
        attn_b.out_q_read = attn_a.out_q_read
        attn_b.block = {-2: attn_a.block[BLOCKS - 2], -1: attn_a.block[BLOCKS - 1]}
        bias_read, bias_ready = {0: [], 1: []}, {}

        def mask_bias(i, g):
            if i == 2:
                return
            if i == 0:
                first, lower, upper = half_block // GRID_R, (8, 24), (24, 32)
            elif i == 1:
                first, lower, upper = 0, (0, 32), (0, 32)
            else:
                first, lower, upper = 0, (0, 8), (8, 24)
            heads = slice(4 * g, 4 * g + 4)
            view = lambda t, a, b: t[:, heads, :].rearrange("p h (j r) -> p h j r", r=GRID_R)[:, :, a:b, :]
            token = None
            for n, ((a, b), sign, base) in enumerate(((lower, 1, GRID_R - 1), (upper, -1, (WIN_W - 1) * GRID_R))):
                in_place = i == 1 and n == 1
                dst_v = view(masked_bias, a - first, b - first)
                src_v = view(masked_bias, a, b) if in_place else view(rel_bias, a, b)
                token = q.issue("gpsimd", lambda e, dst_v=dst_v, src_v=src_v, a=a, b=b, sign=sign, base=base: e.affine_select(
                    out=dst_v, in_=src_v, compare_op=ALU.is_ge, fill=-MASKED, base=base + sign * GRID_R * a,
                    pattern=[[0, 4], [sign * GRID_R, b - a], [0, GRID_R]], channel_multiplier=-sign),
                    after=[bias_here, *bias_read[g], token])
            bias_ready[g] = token

        def add_rel_bias(i, h, scores, dst, after):
            n = scores.shape[1]
            token = q.issue("vector", lambda e: e.scalar_tensor_tensor(dst, scores, SCALE, masked_bias[:, h, 0:n], ALU.mult, ALU.add),
                            after=[*after, bias_ready[h // 4]])
            bias_read[h // 4] = [token]
            if h % 4 == 3 and i + 1 < BLOCKS:
                mask_bias(i + 1, h // 4)
            return token

        attn_b.add_bias = add_rel_bias

        def act_y(hi, lo):
            return lambda k: (hi[:, k, :], lo[:, k, :])

        merged_ready = [()] * KT
        gate_state = {}

        def gate_job(m, n, bias_col, buffer, after):
            result = dense_h()
            slot, temp, free = temps.take()
            z = scaled(result, temp[:, :], after=free)
            token = q.issue("scalar", lambda e: e.activation(buffer[:, n, :], temp[:, :], ACT.Sigmoid, bias=gate_bias[:, bias_col:bias_col + 1]),
                            after=[z, gate_bias_in, *after, *gate_state.get(n, ())])
            release(slot, token)
            gate_state[n] = (token,)

        def merge_a(m, n):
            slot, bank, done = dense(4, n * P, act_y(attn_a.y_hi, attn_a.y_lo), lambda k: attn_a.out_ready, last_of_unit=n == 1)
            token = q.issue("vector", lambda e: e.tensor_tensor(x[:, m, :], bank[:, :], gates[:, n, :], ALU.mult),
                            after=[done, *gate_state[n], *barrier_x])
            release(slot, token)
            gate_state[n] = (token,)
            merged_ready[m] = (token,)

        barrier_x = [rms_state["sum"]] + [t for m in range(KT) for t in h_ready[m]]
        mask_bias(0, 0)
        mask_bias(0, 1)
        start_beside(attn_b.steps(first=7, period=10, delay=11))
        for m in range(0, KT, 2):
            for n in range(2):
                gate_job(m + n, n, m + n, gates, after_a)
            for n in range(2):
                merge_a(m + n, n)
        finish_beside()

        after_b = barrier()
        gate_state.clear()

        def merge_b(m, n):
            slot, bank, done = dense(4, n * P, act_y(qb_hi, qb_lo), lambda k: attn_b.out_ready, last_of_unit=n == 1)
            tslot, temp, tfree = temps.take()
            grid = lambda ap: ap.rearrange("p (r c) -> p r c", r=GRID_R)
            part = q.issue("vector", lambda e: e.tensor_tensor(
                grid(temp[:, :]), bank[:, :].rearrange("p (c r) -> p r c", r=GRID_R), grid(gates_b[:, n, :]), ALU.mult),
                after=[done, *gate_state[n], *tfree])
            release(slot, part)
            gate_state[n] = (part,)
            total = q.issue("vector", lambda e: e.tensor_tensor(temp[:, :], temp[:, :], x[:, m, :], ALU.add), after=[part, *merged_ready[m]])
            merged_ready[m] = split_into(temp[:, :], mg_hi[:, m, :], mg_lo[:, m, :], [total])
            release(tslot, *merged_ready[m])
            x_written[m] = (q.dma("gpsimd", lambda e: e.dma_start(x[:, m, :], dram["x"][m * P:(m + 1) * P, :]), x_back[m], after=[total]),)

        lo_engine[0] = "vector"
        for m in range(0, KT, 2):
            for n in range(2):
                gate_job(m + n, n, KT + m + n, gates_b, after_b)
            for n in range(2):
                merge_b(m + n, n)

        def residual(m, result, factor):
            slot, bank, done = result
            token = q.issue("vector", lambda e: e.scalar_tensor_tensor(x[:, m, :], bank[:, :], factor, x[:, m, :], ALU.mult, ALU.add),
                            after=[done, *x_written[m]])
            release(slot, token)
            x_written[m] = (token,)

        def out_projection(act, ready, gain):
            for m in range(KT):
                residual(m, dense(KT, 0, act, ready), 1.0)
                norm_tile(m, gain)

        out_projection(lambda k: (mg_hi[:, k, :], mg_lo[:, k, :]), lambda k: merged_ready[k], 1)

        def mlp(n_tiles, hidden_tile, after, factor, norm):
            ring = Ring([(act_hi[:, n, :], act_lo[:, n, :]) for n in range(ff_ring)])
            ring.users = [tuple(after)] * ff_ring

            def take_hidden():
                slot, (hi, lo), free = ring.take()
                return slot, (hi, lo), hidden_tile(hi, lo, free)

            sizes = [min(FF_CHUNK, n_tiles - s) for s in range(0, n_tiles, FF_CHUNK)]
            held = []

            for c, size in enumerate(sizes):
                if len(held) == c:
                    held.append([])
                while len(held[c]) < size:
                    held[c].append(take_hidden())
                if c + 1 < len(sizes):
                    held.append([take_hidden()])
                tiles = held[c]
                results = []
                if c == len(sizes) - 1:
                    results = dense_pair(size, lambda k: tiles[k][1], lambda k: tiles[k][2])
                for m in range(KT):
                    result = results.pop(0) if results else dense(size, 0, lambda k: tiles[k][1], lambda k: tiles[k][2])
                    residual(m, result, factor)
                    if c == len(sizes) - 1:
                        norm(m)
                for slot, _, _ in tiles:
                    release(slot, result[2])

        def relu_squared(hi, lo, free):
            result = dense_h()
            slot, bank, done = result
            s1, positive, f1 = temps.take()
            token = q.issue("vector", lambda e: e.scalar_tensor_tensor(positive[:, :], bank[:, :], 0.0, rms_inv[:, :], ALU.max, ALU.mult),
                            after=[done, rms_state["ready"], *f1])
            release(slot, token)
            s2, squared, f2 = temps.take()
            square = q.issue("scalar", lambda e: e.activation(squared[:, :], positive[:, :], ACT.Square), after=[token, *f2])
            release(s1, square)
            tokens = split_into(squared[:, :], hi, lo, [square], hi_after=free)
            release(s2, *tokens)
            return tokens

        def swiglu(hi, lo, free):
            gate = dense_h()
            s1, temp, f1 = temps.take()
            g = scaled(gate, temp[:, :], after=f1)
            s2, act, f2 = temps.take()
            silu = q.issue("scalar", lambda e: e.activation(act[:, :], temp[:, :], ACT.Silu), after=[g, *f2])
            release(s1, silu)
            up = dense_h()
            s3, value, f3 = temps.take()
            v = scaled(up, value[:, :], after=f3)
            product = q.issue("vector", lambda e: e.tensor_tensor(value[:, :], value[:, :], act[:, :], ALU.mult), after=[v, silu])
            release(s2, product)
            tokens = split_into(value[:, :], hi, lo, [product], hi_after=free)
            release(s3, *tokens)
            return tokens

        pending_norm[0] = norm_finish
        for_both = q.issue("vector", lambda e: e.tensor_tensor(gain_product[:, :], gains[:, 2, :], gains[:, 3, :], ALU.mult),
                           after=[gains_in])

        def norm_tile_twice(m):
            q.wait("scalar", for_both)
            q.wait("vector", for_both)
            h_tile(m, gain_product[:, m:m + 1])
            square_tile(m)
            square_tile(m, scaled_square_sum, "sum_scaled", gains[:, 2, m:m + 1])

        mlp(FF1_TILES, relu_squared, barrier(), 1.0, norm_tile_twice)

        def rescale(m):
            x_written[m] = (q.issue("vector", lambda e: e.scalar_tensor_tensor(
                x[:, m, :], x[:, m, :], gains[:, 2, m:m + 1], rms_first[:, :], ALU.mult, ALU.mult),
                after=[*x_written[m], *h_ready[m], rms_state["first"], rms_state["sum"], rms_state["sum_scaled"]]),)

        def norm_and_rescale():
            first_scale = norm_finish_twice()
            start_beside([(12, first_scale)] + [(16 + 4 * m, lambda m=m: rescale(m)) for m in range(KT)])

        pending_norm[0] = norm_and_rescale

        with_gain = KT // 2
        last_squares = []

        def output_norm_tile(m):
            if m < KT - 1:
                square_tile(m)
            else:
                _, temp, free = temps.take()
                last_squares[:] = [temp, q.issue("scalar", lambda e: e.activation(temp[:, :], x[:, m, :], ACT.Square),
                                                 after=[*x_written[m], *free])]
            if m < with_gain:
                x_written[m] = (q.issue("scalar", lambda e: e.activation(x[:, m, :], x[:, m, :], ACT.Copy, scale=gains[:, 9, m:m + 1]),
                                        after=[*x_written[m], *h_ready[m], rms_state["sum"]]),)
            if m == KT - 2:
                q.issue("scalar", lambda e: e.activation(root_ready[:, :], eps_col[:, :], ACT.Sqrt), after=[eps_ready], signal=False)

        for layer in range(LAYERS_2):
            base = 3 + 3 * layer
            if layer > 0:
                pending_norm[0] = norm_finish
            mlp(FF2_TILES, swiglu, () if layer == 0 else barrier(), 0.5, lambda m: norm_tile(m, base + 1))
            start = barrier()
            dist2_in = load_const(2, dist_2[:, :], dram["dist_2"], after=start)
            padded = q.issue("vector", lambda e: e.memset(conv_u[:, 0:2], 0.0), after=start)
            attn = Attention(values=v2, probs=probs_2, turned=probs_t2, out_q=out_q2, key_range=window_2, chunks=chunks_2,
                             add_bias=alibi(dist_2, dist2_in, BLOCK), sink=1 + layer, **gqa_parts(q2, k2_hi, k2_lo))
            pending_norm[0] = norm_finish
            attn.inputs_ready, attn.values_ready = qkv_gqa(q2, k2_hi, k2_lo, v2, after=start)
            attn.probs_ring.users = [tuple(start)] * 3
            attn.turned_ring.users = [tuple(start)] * 2
            conv = {"c": start, "u": [padded], "y": start}
            cat_ready = []

            def conv_c_job():
                conv["c"] = [scaled(dense_h(), conv_c[:, :], after=conv["c"])]

            def conv_h_job(f, layer=layer):
                slot, temp, free = temps.take()
                hz = scaled(dense_h(), temp[:, :], after=free)
                u = q.issue("gpsimd", lambda e: e.tensor_tensor(conv_u[:, 2:TOKENS + 2], temp[:, :], conv_c[:, :], ALU.mult),
                            after=[hz, *conv["c"], *conv["u"]])
                release(slot, u)
                conv["c"] = [u]
                w = lambda k: conv_w[:, layer, f, k:k + 1]

                def own_token():
                    conv["y"] = [q.issue("scalar", lambda e: e.activation(conv_y[:, :], conv_u[:, 2:TOKENS + 2], ACT.Copy, scale=w(2)),
                                         after=[u, padded, conv_w_in, *conv["y"]])]

                def earlier_tokens():
                    for k in (1, 0):
                        conv["y"] = [q.issue("vector", lambda e, k=k: e.scalar_tensor_tensor(
                            conv_y[:, :], conv_u[:, k:k + TOKENS], w(k), conv_y[:, :], ALU.mult, ALU.add), after=[*conv["y"], u, padded])]
                    conv["u"] = list(conv["y"])
                later(3, own_token)
                later(5, earlier_tokens)

            def conv_b_job(f, start=start):
                slot, temp, free = temps.take()
                bz = scaled(dense_h(), temp[:, :], after=free)
                o = q.issue("gpsimd", lambda e: e.tensor_tensor(temp[:, :], temp[:, :], conv_y[:, :], ALU.mult), after=[bz, *conv["y"]])
                conv["y"] = [o]
                cat_ready.append([])
                later(3, lambda: split_later(slot, temp[:, :], cv_hi[:, f, :], cv_lo[:, f, :], cat_ready[f], [o, *start]))

            lo_engine[0] = "gpsimd"
            start_beside(attn.steps(first=5, period=10, delay=11))
            for f in range(4):
                conv_c_job()
                conv_h_job(f)
                conv_b_job(f)
            finish_beside()
            lo_engine[0] = "vector"
            cat = [(cv_hi[:, f, :], cv_lo[:, f, :], cat_ready[f]) for f in range(4)]
            cat[3:3] = [(attn.y_hi[:, t, :], attn.y_lo[:, t, :], attn.out_ready) for t in range(4)]
            out_projection(lambda k: cat[k][:2], lambda k: cat[k][2], base + 2)
            pending_norm[0] = norm_finish
            last = layer == LAYERS_2 - 1
            mlp(FF2_TILES, swiglu, barrier(), 0.5, output_norm_tile if last else lambda m: norm_tile(m, base + 3))

        _, bank, free = value_bank.take()
        for n, (source, ready) in enumerate(((square_sum, rms_state["sum"]), last_squares)):
            summed = q.issue("tensor", lambda e, n=n, source=source: e.matmul(
                bank[:, :], ones[:, :], source[:, :], start=n == 0, stop=n == 1), after=[ready, ones_ready, *free], signal=n == 1)
        _, roots, free = temps.take()
        root = q.issue("scalar", lambda e: e.activation(roots[:, :], bank[:, :], ACT.Sqrt, bias=eps_col[:, :], scale=1 / D_MODEL),
                       after=[summed, *free])
        stores = []
        output_order = [m for pair in range(0, KT // 2, 2) for first in (KT // 2 + pair, pair) for m in (first, first + 1)]
        for cols in (slice(0, TOKENS // 2), slice(TOKENS // 2, TOKENS)):
            inverse = q.issue("vector", lambda e, cols=cols: e.reciprocal(rms_inv[:, cols], roots[:, cols]),
                              after=[root, rms_state["ready"]])
            for m in output_order:
                if m < with_gain:
                    done = q.issue("gpsimd", lambda e, m=m, cols=cols: e.tensor_tensor(
                        x[:, m, cols], x[:, m, cols], rms_inv[:, cols], ALU.mult), after=[*x_written[m], inverse])
                else:
                    done = q.issue("vector", lambda e, m=m, cols=cols: e.scalar_tensor_tensor(
                        x[:, m, cols], x[:, m, cols], gains[:, 9, m:m + 1], rms_inv[:, cols], ALU.mult, ALU.mult),
                        after=[*x_written[m], inverse, summed])
                if m % 2 == 1:
                    stores.append(q.dma("sync", lambda e, m=m, cols=cols: e.dma_start(
                        out[(m - 1) * P:(m + 1) * P, cols].rearrange("(t p) n -> p t n", p=P), x[:, m - 1:m + 1, cols]),
                        out_stored, after=[done]))
        q.wait("sync", stores[-1])
        assert current[0] == len(units)

        block = stack.enter_context(nc.Block())
        for name in engines:
            def program(engine, name=name):
                for instruction in q.todo[name]:
                    instruction(engine)
            in_block = {"tensor": block.tensor, "vector": block.vector, "scalar": block.scalar,
                            "gpsimd": block.gpsimd, "sync": block.sync}[name]
            in_block(program)


def plan_units(dram):
    units = []

    def column_tiles(w, tiles):
        units.extend((w[t].rearrange("p k n -> p (k n)"), w.shape[2] * w.shape[3]) for t in tiles)

    def down(w, chunk, size):
        for m in range(KT):
            src = w[m, :, chunk * FF_CHUNK:chunk * FF_CHUNK + size, :].rearrange("p k n -> p (k n)")
            units.append((src, size * P))

    def mlp(ups, w_down, n_tiles):
        n_chunks = -(-n_tiles // FF_CHUNK)
        done = 0
        for c in range(n_chunks):
            size = min(FF_CHUNK, n_tiles - c * FF_CHUNK)
            until = min(n_tiles, c * FF_CHUNK + size + 1)
            for t in range(done, until):
                for w in ups:
                    column_tiles(w, [t])
            done = until
            down(w_down, c, size)

    column_tiles(dram["w_in"], range(18))
    for pair in range(KT // 2):
        column_tiles(dram["w_in"], [18 + 2 * pair, 19 + 2 * pair])
        column_tiles(dram["w_proj_a"], [pair])
    for pair in range(KT // 2):
        column_tiles(dram["w_in"], [26 + 2 * pair, 27 + 2 * pair])
        column_tiles(dram["w_proj_b"], [pair])
    column_tiles(dram["w_out"], range(KT))
    mlp([dram["w_up"]], dram["w_down"], FF1_TILES)
    for layer in range(LAYERS_2):
        mlp([dram["ffn1_wg"][layer], dram["ffn1_wu"][layer]], dram["ffn1_wd"][layer], FF2_TILES)
        column_tiles(dram["w_in_2"][layer], range(18))
        column_tiles(dram["w_out_2"][layer], range(KT))
        mlp([dram["ffn2_wg"][layer], dram["ffn2_wu"][layer]], dram["ffn2_wd"][layer], FF2_TILES)
    return units



def tiled(w, width=P, columns=None, rows=None):
    if rows is not None:
        w = w[rows]
    if columns is not None:
        w = w[:, columns]
    k, n = w.shape
    return np.ascontiguousarray(w.reshape(k // P, P, n // width, width).transpose(2, 1, 0, 3))


def head_order():
    return np.concatenate([np.arange(HEAD) + HEAD * h for m in range(GROUP) for h in (m, m + GROUP)])


def distances():
    query = np.arange(BLOCK)[:, None]
    both = np.abs(query + BLOCK - np.arange(3 * BLOCK)[None, :])
    past = query + BLOCK - np.arange(2 * BLOCK)[None, :]
    return (np.where(both <= BLOCK, both, MASKED).astype(np.float32),
            np.where((past >= 0) & (past < BLOCK), past, MASKED).astype(np.float32))


def kernel(**inputs):
    import concourse.bacc as bacc
    from concourse.bass_utils import run_bass_kernel_spmd

    a = {name: np.asarray(value) for name, value in inputs.items()}
    order = head_order()
    width = HEADS * HEAD
    kv = KV_HEADS * HEAD
    at = np.arange(a["w_in"].shape[2])
    b0 = width + 2 * kv
    cols_1 = [at[width:width + kv], at[width + kv:b0], order]
    for t in range(4):
        cols_1 += [at[b0 + 2 * width + t * P:b0 + 2 * width + (t + 1) * P], at[b0 + width + t * P:b0 + width + (t + 1) * P]]
    cols_1 += [at[b0:b0 + width], at[b0 + 3 * width:]]
    at2 = np.arange(a["w_in_2"].shape[2])
    cols_2 = [at2[width:width + kv], at2[width + kv:b0], order]
    for f in range(4):
        b, c, h = (b0 + n * width + f * P for n in range(3))
        cols_2 += [at2[c:c + P], at2[h:h + P], at2[b:b + P]]
    cols_1, cols_2 = np.concatenate(cols_1), np.concatenate(cols_2)
    rows_2 = np.concatenate([np.arange(width, 2 * width - P), order, np.arange(2 * width - P, 2 * width)])
    both = lambda f, w: np.stack([f(w[layer]) for layer in range(LAYERS_2)])
    column = lambda g: g.reshape(-1, P).T
    gains = [a["norm_mix"][0], a["norm_mlp"][0], a["norm_final"]]
    for layer in range(LAYERS_2):
        gains += [a[n][layer] for n in ("ffn1_norm_2", "mix_norm_2", "ffn2_norm_2")]
    gains.append(a["final_norm_2"])
    dist_1, dist_2 = distances()
    arrays = {
        "x": a["x"][0].T,
        "gains": np.stack([column(g) for g in gains], axis=1),
        "dist_1": dist_1, "dist_2": dist_2, "identity": np.eye(P, dtype=np.float32),
        "gate_bias": column(a["b_gate"][0]),
        "sinks": np.concatenate([a["sink"], a["attn_sink_2"]]),
        "conv_w": a["conv_w_2"].reshape(LAYERS_2, 3, 4, P).transpose(3, 0, 2, 1),
        "rpb": a["rpb"][0],
        "w_in": tiled(a["w_in"][0], columns=cols_1),
        "w_proj_a": tiled(a["w_proj_a"][0], 2 * P, rows=order),
        "w_proj_b": tiled(a["w_proj_b"][0], 2 * P),
        "w_out": tiled(a["w_out"][0]),
        "w_up": tiled(a["w_up"][0]), "w_down": tiled(a["w_down"][0]),
        "w_in_2": both(lambda w: tiled(w, columns=cols_2), a["w_in_2"]),
        "w_out_2": both(lambda w: tiled(w, rows=rows_2), a["w_out_2"]),
    }
    for n in ("ffn1", "ffn2"):
        for w in ("wg", "wu", "wd"):
            arrays[f"{n}_{w}"] = both(tiled, a[f"{n}_{w}_2"])
    arrays = {name: np.ascontiguousarray(v) for name, v in arrays.items()}

    nc = bacc.Bacc("TRN2", target_bir_lowering=False, num_devices=1)
    dram = {name: nc.dram_tensor(f"{name}_dram", v.shape, mybir.dt.from_np(v.dtype), kind="ExternalInput").ap()
            for name, v in arrays.items()}
    dram["rel_scratch"] = nc.dram_tensor("rel_scratch_dram", (GRID_R * HEADS, REL_PAD), F32, kind="Internal").ap()
    out = nc.dram_tensor("out_dram", (D_MODEL, TOKENS), F32, kind="ExternalOutput").ap()
    two_blocks(nc, dram, out)
    result = run_bass_kernel_spmd(nc, [{f"{name}_dram": v for name, v in arrays.items()}], core_ids=[0])
    return np.ascontiguousarray(result.results[0]["out_dram"].T)[None]
```
